# Optimizing a Trainium2 kernel written in Bass

```python
import jax, jax.numpy as jnp
from jax import lax
import numpy as np

D_MODEL = 2048
BATCH = 1
SEQ = 256
DEPTH = 1

CHUNK = 64
Q_BLOCK = 128
N_MEM = 256
EPS = 1e-6

D_CONV = D_MODEL
CONV_K = 31

MLA_HEADS = 16
Q_LORA = 512
KV_LORA = 512
QK_NOPE = 128
QK_ROPE = 64
V_DIM = 128
ROPE_THETA = 10000.0

X_HEADS = 4
X_HEAD_DIM = 128

D_FF = 4 * D_MODEL

N_BRANCH = 2
IN_SIZES = (2 * D_CONV, Q_LORA, KV_LORA, QK_ROPE, N_BRANCH * D_MODEL)
IN_COLS = sum(IN_SIZES)
IN_SPLITS = tuple(int(v) for v in np.cumsum(IN_SIZES)[:-1])

kernel_name = "hybrid_conformer_mla_gated_encoder"

def rms_norm(x, g):
    x32 = x.astype(jnp.float32)
    y = x32 * lax.rsqrt(jnp.mean(x32 * x32, axis=-1, keepdims=True) + EPS)
    return (y * g.astype(jnp.float32)).astype(x.dtype)

def layer_norm(x, g, b):
    x32 = x.astype(jnp.float32)
    mu = jnp.mean(x32, axis=-1, keepdims=True)
    xc = x32 - mu
    y = xc * lax.rsqrt(jnp.mean(xc * xc, axis=-1, keepdims=True) + EPS)
    return (y * g.astype(jnp.float32) + b.astype(jnp.float32)).astype(x.dtype)

def rope_tables(positions):
    inv_freq = 1.0 / (ROPE_THETA ** (jnp.arange(0, QK_ROPE, 2, dtype=jnp.float32) / QK_ROPE))
    ang = positions.astype(jnp.float32)[..., None] * inv_freq
    return jnp.cos(ang), jnp.sin(ang)

def apply_rope(x, cos, sin):
    x32 = x.astype(jnp.float32)
    x1, x2 = jnp.split(x32, 2, axis=-1)
    out = jnp.concatenate([x1 * cos - x2 * sin, x2 * cos + x1 * sin], axis=-1)
    return out.astype(x.dtype)

def conformer_conv_branch(u, conv_w, conv_b, ln_g, ln_b, w_pw2):
    a, gate = jnp.split(u, 2, axis=-1)
    h = a * jax.nn.sigmoid(gate)
    h = lax.conv_general_dilated(
        h, conv_w[:, None, :], window_strides=(1,), padding=[(CONV_K - 1, 0)],
        dimension_numbers=("NWC", "WIO", "NWC"), feature_group_count=D_CONV) + conv_b
    h = jax.nn.silu(layer_norm(h, ln_g, ln_b))
    return h @ w_pw2

def chunk_causal_attention(q, k, v):
    B, S, H, Dk = q.shape
    nb = S // Q_BLOCK
    scale = Dk ** -0.5
    q_blocks = q.reshape(B, nb, Q_BLOCK, H, Dk).transpose(1, 0, 2, 3, 4)
    k_chunk = jnp.arange(S) // CHUNK

    def one_block(args):
        q_blk, blk = args
        s = jnp.einsum("bqhd,bkhd->bhqk", q_blk, k, preferred_element_type=jnp.float32) * scale
        q_chunk = (blk * Q_BLOCK + jnp.arange(Q_BLOCK)) // CHUNK
        mask = k_chunk[None, :] <= q_chunk[:, None]
        s = jnp.where(mask[None, None], s, -jnp.inf)
        p = jax.nn.softmax(s, axis=-1).astype(v.dtype)
        return jnp.einsum("bhqk,bkhd->bqhd", p, v)

    o = lax.map(one_block, (q_blocks, jnp.arange(nb)))
    return o.transpose(1, 0, 2, 3, 4).reshape(B, S, H, v.shape[-1])

def mla_branch(c_q, c_kv, k_pe, cos, sin, q_norm_g, w_uq, kv_norm_g, w_ukv, w_o):
    B, S, _ = c_q.shape
    q = (rms_norm(c_q, q_norm_g) @ w_uq).reshape(B, S, MLA_HEADS, QK_NOPE + QK_ROPE)
    q_nope, q_pe = q[..., :QK_NOPE], q[..., QK_NOPE:]
    q_pe = apply_rope(q_pe, cos[:, :, None, :], sin[:, :, None, :])
    kv = (rms_norm(c_kv, kv_norm_g) @ w_ukv).reshape(B, S, MLA_HEADS, QK_NOPE + V_DIM)
    k_nope, v = kv[..., :QK_NOPE], kv[..., QK_NOPE:]
    k_pe = apply_rope(k_pe, cos, sin)
    q_full = jnp.concatenate([q_nope, q_pe], axis=-1)
    k_full = jnp.concatenate(
        [k_nope, jnp.broadcast_to(k_pe[:, :, None, :], (B, S, MLA_HEADS, QK_ROPE))], axis=-1)
    o = chunk_causal_attention(q_full, k_full, v)
    return o.reshape(B, S, MLA_HEADS * V_DIM) @ w_o

def memory_cross_attention(h, mem_n, w_xq, w_xkv, w_xo):
    B, S, _ = h.shape
    q = (h @ w_xq).reshape(B, S, X_HEADS, X_HEAD_DIM)
    kv = (mem_n @ w_xkv).reshape(B, mem_n.shape[1], 2, X_HEADS, X_HEAD_DIM)
    k, v = kv[:, :, 0], kv[:, :, 1]
    s = jnp.einsum("bqhd,bmhd->bhqm", q, k, preferred_element_type=jnp.float32) * (X_HEAD_DIM ** -0.5)
    p = jax.nn.softmax(s, axis=-1).astype(v.dtype)
    o = jnp.einsum("bhqm,bmhd->bqhd", p, v).reshape(B, S, X_HEADS * X_HEAD_DIM)
    return o @ w_xo

def squared_relu_mlp(h, w1, w2):
    return jnp.square(jax.nn.relu(h @ w1)) @ w2

def setup_inputs(seed: int = 0) -> dict:
    key = jax.random.key(seed)
    ks = iter(jax.random.split(key, 40))

    def w(shape, fan_in):
        return jax.random.normal(next(ks), shape, jnp.float32) * (fan_in ** -0.5)

    def gain(shape):
        return 1.0 + 0.02 * jax.random.normal(next(ks), shape, jnp.float32)

    def bias(shape):
        return 0.02 * jax.random.normal(next(ks), shape, jnp.float32)

    L = DEPTH
    return {
        "x": jax.random.normal(next(ks), (BATCH, SEQ, D_MODEL), jnp.float32),
        "mem": jax.random.normal(next(ks), (BATCH, N_MEM, D_MODEL), jnp.float32),
        "positions": jnp.broadcast_to(jnp.arange(SEQ, dtype=jnp.int32), (BATCH, SEQ)),
        "norm_mix_g": gain((L, D_MODEL)),
        "w_in": w((L, D_MODEL, IN_COLS), D_MODEL),
        "b_gate": bias((L, N_BRANCH * D_MODEL)),
        "conv_w": w((L, CONV_K, D_CONV), CONV_K),
        "conv_b": bias((L, D_CONV)),
        "conv_ln_g": gain((L, D_CONV)),
        "conv_ln_b": bias((L, D_CONV)),
        "w_conv_out": w((L, D_CONV, D_MODEL), D_CONV),
        "q_norm_g": gain((L, Q_LORA)),
        "w_uq": w((L, Q_LORA, MLA_HEADS * (QK_NOPE + QK_ROPE)), Q_LORA),
        "kv_norm_g": gain((L, KV_LORA)),
        "w_ukv": w((L, KV_LORA, MLA_HEADS * (QK_NOPE + V_DIM)), KV_LORA),
        "w_mla_out": w((L, MLA_HEADS * V_DIM, D_MODEL), MLA_HEADS * V_DIM),
        "w_out": w((L, D_MODEL, D_MODEL), D_MODEL),
        "norm_mem_g": gain((L, D_MODEL)),
        "mem_norm_g": gain((L, D_MODEL)),
        "w_xq": w((L, D_MODEL, X_HEADS * X_HEAD_DIM), D_MODEL),
        "w_xkv": w((L, D_MODEL, 2 * X_HEADS * X_HEAD_DIM), D_MODEL),
        "w_xo": w((L, X_HEADS * X_HEAD_DIM, D_MODEL), X_HEADS * X_HEAD_DIM),
        "norm_ffn_g": gain((L, D_MODEL)),
        "w_ff1": w((L, D_MODEL, D_FF), D_MODEL),
        "w_ff2": w((L, D_FF, D_MODEL), D_FF),
        "final_norm_g": gain((D_MODEL,)),
    }

def reference(x, mem, positions, norm_mix_g, w_in, b_gate, conv_w, conv_b, conv_ln_g, conv_ln_b,
              w_conv_out, q_norm_g, w_uq, kv_norm_g, w_ukv, w_mla_out, w_out,
              norm_mem_g, mem_norm_g, w_xq, w_xkv, w_xo, norm_ffn_g, w_ff1, w_ff2, final_norm_g):
    B, S, D = x.shape
    cos, sin = rope_tables(positions)
    for l in range(DEPTH):
        h = rms_norm(x, norm_mix_g[l])
        z = h @ w_in[l]
        u_conv, c_q, c_kv, k_pe, gate_logits = jnp.split(z, IN_SPLITS, axis=-1)
        y_conv = conformer_conv_branch(u_conv, conv_w[l], conv_b[l], conv_ln_g[l], conv_ln_b[l],
                                       w_conv_out[l])
        y_mla = mla_branch(c_q, c_kv, k_pe, cos, sin, q_norm_g[l], w_uq[l], kv_norm_g[l],
                           w_ukv[l], w_mla_out[l])
        gates = jax.nn.sigmoid(gate_logits + b_gate[l]).reshape(B, S, N_BRANCH, D)
        merged = gates[:, :, 0, :] * y_conv + gates[:, :, 1, :] * y_mla
        x = x + merged @ w_out[l]
        x = x + memory_cross_attention(rms_norm(x, norm_mem_g[l]), rms_norm(mem, mem_norm_g[l]),
                                       w_xq[l], w_xkv[l], w_xo[l])
        x = x + squared_relu_mlp(rms_norm(x, norm_ffn_g[l]), w_ff1[l], w_ff2[l])
    return rms_norm(x, final_norm_g)


_drawn_inputs = setup_inputs


def setup_inputs(seed=0):
    import zlib

    import numpy as np

    out = dict(_drawn_inputs(seed))
    spreads = {}
    factors = {'norm_mix_g': 6.564,
     'b_gate': 8.0,
     'conv_b': 3.772,
     'conv_ln_g': 6.966,
     'conv_ln_b': 8.0,
     'q_norm_g': 8.0,
     'kv_norm_g': 8.0,
     'norm_mem_g': 8.0,
     'mem_norm_g': 8.0,
     'norm_ffn_g': 9.747,
     'final_norm_g': 8.089}
    for name, (base, spread) in spreads.items():
        noise = np.random.default_rng([zlib.crc32(name.encode()), seed]).standard_normal(out[name].shape)
        drawn = base * np.exp(spread * noise) if base else spread * noise
        out[name] = __import__('jax').numpy.asarray(drawn.astype(out[name].dtype))
    for name, factor in factors.items():
        out[name] = (out[name] * factor).astype(out[name].dtype)
    return out
```

```python
from contextlib import ExitStack

import numpy as np

import concourse.bass as bass
from concourse import mybir

ALU = mybir.AluOpType
ACT = mybir.ActivationFunctionType
AX_X = mybir.AxisListType.X
F32 = mybir.dt.float32
F32R = mybir.dt.float32r
I32 = mybir.dt.int32
ds = bass.ds

P = 128
D = 2048
SEQ = 256
TT = SEQ // P
KT = D // P
NC = 512
CH = D // NC
CPB = NC // P
CONV_K = 31
PAD = CONV_K - 1
HC = SEQ + PAD
LORA = 512
LT = LORA // P
NOPE, ROPE, VD = 128, 64, 128
HALF = ROPE // 2
HEADS = 16
PAIRS = HEADS // 2
QW = 2 * (NOPE + ROPE)
KVW = 2 * (NOPE + VD)
XH = 4
DFF = 4 * D
SW = P + SEQ
SCORES = [(0, 0, P), (0, P, SW), (1, 0, P), (1, P, SW)]
GROUPS = DFF // D
EPS = 1e-6
NEG = -3.0e38
SM = float(NOPE + ROPE) ** -0.5
XSM = 128.0 ** -0.5
COL_A, COL_G, COL_CQ, COL_CKV = 0, D, 2 * D, 2 * D + LORA
COL_KPE = COL_CKV + LORA
COL_GATE = COL_KPE + ROPE

UE = 2 * NC
RING = 4
LEAD = 3
UPC = KT // 2
U_CONV = 0
U_LORA = U_CONV + 2 * CH * UPC
U_KPE = U_LORA + 2 * UPC
U_ATT = U_KPE + 1
ATT_UNITS = 4 + UPC
U_MLA = U_ATT + PAIRS * ATT_UNITS
U_XKV = U_MLA + CH * UPC
U_COUT = U_XKV + 2 * UPC
U_WOUT = U_COUT + CH * UPC
U_XQ = U_WOUT + CH * UPC
U_XO = U_XQ + UPC
U_FF = U_XO + CH * 2
FF_UNITS = 2 * CH * UPC
U_END = U_FF + GROUPS * FF_UNITS

T_X = 0
T_CONV = T_X + CH
T_CQ = T_CONV + CH
T_CKV = T_CQ + 1
T_MEM = T_CKV + 1
T_XK = T_MEM + CH
T_MRG = T_XK + 1
T_X1 = T_MRG + CH
T_XQ = T_X1 + CH
T_X2 = T_XQ + 1
T_FF = T_X2 + CH


def splits_before(turn):
    return turn - CH * (turn > T_CONV) - (turn > T_XK) - (turn > T_XQ)


N_CONV = 0
N_CQ = N_CONV + CH
N_CKV = N_CQ + 1
N_GATE = N_CKV + 1
N_MLA = N_GATE + PAIRS
N_XK = N_MLA + CH
N_XV = N_XK + 1
N_COUT = N_XV + 1
N_WOUT = N_COUT + CH
N_XQ = N_WOUT + CH
N_XO = N_XQ + 1
N_FF = N_XO + CH

R_X, R_Q, R_KV, R_MEM, R_1, R_2, R_3 = range(1, 8)
SS_X = TT
SS_Q = SS_X + TT
SS_KV = SS_Q + TT
SS_MEM = SS_KV + TT * CH
SS_1 = SS_MEM + TT * CH
SS_2 = SS_1 + TT * CH
SS_3 = SS_2 + TT * CH
CONV_STEPS = CONV_K + 2


def pair_of(n):
    return (n + 1) % 2


V_MIX, V_LG, V_LB, V_NMEM, V_MEMN, V_FFN = (KT * n for n in range(6))
V_QG = 6 * KT
V_KG = V_QG + LT
V_N = V_KG + LT

PI_NUM, PI_DEN = 31415926535897932384626433832795028841971693993751058209749445923, 10 ** 64
MAGIC = 1.5 * 2.0 ** 23
TWO_PI = 6.283185


def turn_pieces(n):
    num, den, out = PI_DEN, 2 * PI_NUM, []
    for k in range(n):
        bits = 14 + 12 * k
        piece = (num << bits) // den
        out.append(piece / 2.0 ** bits)
        num, den = (num << bits) - piece * den, den << bits
    return out


def inv_freqs():
    exponent = np.arange(0, ROPE, 2, dtype=np.float32) / np.float32(ROPE)
    return [float(v) for v in np.float32(1.0) / np.power(np.float32(10000.0), exponent)]


def nbytes(shape):
    n = 4
    for s in shape[1:]:
        n *= s
    return n


def build(nc, x, mem, positions, norm_mix_g, w_in, b_gate, conv_w, conv_b, conv_ln_g, conv_ln_b,
          w_conv_out, q_norm_g, w_uq, kv_norm_g, w_ukv, w_mla_out, w_out, norm_mem_g, mem_norm_g,
          w_xq, w_xkv, w_xo, norm_ffn_g, w_ff1, w_ff2, final_norm_g, out):
    def k_rows(w):
        return w.rearrange("o (k p) n -> p (o k) n", p=P)

    w_in, w_uq, w_ukv, w_mla_out, w_conv_out, w_out = (k_rows(w) for w in (w_in, w_uq, w_ukv, w_mla_out, w_conv_out, w_out))
    w_xq, w_xkv, w_xo, w_ff1, w_ff2 = (k_rows(w) for w in (w_xq, w_xkv, w_xo, w_ff1, w_ff2))
    x_v, mem_v, out_v = (v.rearrange("o (t p) n -> p (o t) n", p=P) for v in (x, mem, out))

    with ExitStack() as ctx:
        cursor = [(nc.sbuf_base + 31) // 32 * 32]

        def at(offset, name, shape, dt=F32):
            return nc.alloc_sbuf_tensor_at(name, shape, dt, offset=offset)

        def take(name, shape, dt=F32):
            offset = cursor[0]
            cursor[0] += (nbytes(shape) + 31) // 32 * 32
            return at(offset, name, shape, dt)

        KS = nbytes([P, KT, SEQ])
        raw = take("raw", [P, RING, UE])
        whi = take("whi", [P, RING, UE], F32R)
        wlo = take("wlo", [P, RING, UE], F32R)
        o = cursor[0]
        a_hi = take("a_hi", [P, KT, SEQ], F32R)
        a_lo = take("a_lo", [P, KT, SEQ], F32R)
        ln_sq = at(o, "ln_sq", [P, KT, SEQ])
        ln_sum = at(o + KS, "ln_sum", [P, KT // 2, SEQ])
        sq_mem = at(o + KS + KS // 2, "sq_mem", [P, TT, NC])
        o = cursor[0]
        c_hi = take("c_hi", [P, KT, SEQ], F32R)
        c_lo = take("c_lo", [P, KT, SEQ], F32R)
        cw_rows = at(o, "cw_rows", [CONV_K + 1, D])
        sq_x = at(o + nbytes([P, D]), "sq_x", [P, TT, D])
        o = cursor[0]
        gates = take("gates", [P, TT, 2 * D])
        x_in = at(o, "x_in", [P, TT, D])
        vec_rows = at(o + KS, "vec_rows", [P, P])
        rope_tmp = at(o + KS + 512, "rope_tmp", [P, 6, TT * HALF])
        xo_hi = at(o, "xo_hi", [P, XH, SEQ], F32R)
        xo_lo = at(o + 4096, "xo_lo", [P, XH, SEQ], F32R)
        fin_g = at(o + 8192, "fin_g", [P, D])
        fin = at(o + KS, "fin", [P, TT, D])
        o = cursor[0]
        m_hi = take("m_hi", [P, KT, SEQ], F32R)
        m_lo = take("m_lo", [P, KT, SEQ], F32R)
        cq_hi = at(o, "cq_hi", [P, LT, SEQ], F32R)
        cq_lo = at(o + 4096, "cq_lo", [P, LT, SEQ], F32R)
        ckv_hi = at(o + 8192, "ckv_hi", [P, LT, SEQ], F32R)
        ckv_lo = at(o + 12288, "ckv_lo", [P, LT, SEQ], F32R)
        kv_row = at(o + 16384, "kv_row", [P, TT, KVW])
        sq_lat = at(o + 16384, "sq_lat", [P, TT, LORA])
        qT = at(o + 20480, "qT", [P, 2, SEQ])
        kT = at(o + 22528, "kT", [P, 2, SEQ])
        qrT = at(o + 24576, "qrT", [ROPE, 2, SEQ])
        kpeT = at(o + 26624, "kpeT", [ROPE, SEQ])
        mask = at(o + 27648, "mask", [P, SW])
        kpe_row = at(o + 29184, "kpe_row", [P, TT, ROPE])
        kpe_rot = at(o + 29696, "kpe_rot", [P, TT, ROPE])
        rot = at(o + 30208, "rot", [P, 4, 2, TT, HALF])
        xkT = at(o, "xkT", [P, XH, SEQ])
        xv = at(o + 4096, "xv", [P, TT, XH * P])
        xqT = at(o + 8192, "xqT", [P, XH, SEQ])
        xp = at(o + 12288, "xp", [P, XH, TT, SEQ])
        sq_res = at(o + 12288, "sq_res", [P, TT, NC])
        xpT = at(o + 20480, "xpT", [P, XH, TT, SEQ])
        o = cursor[0]
        hconv = take("hconv", [P, KT, HC])
        xres = at(o, "xres", [P, TT, D])
        o = cursor[0]
        acc = take("acc", [P, 2, SEQ])
        mean_w = at(o + 4 * SEQ, "mean_w", [P, P])
        o = cursor[0]
        rows = take("rows", [P, 2, TT, NC])
        q_row = at(o, "q_row", [P, TT, QW])
        pT = at(o, "pT", [P, 2, SW])
        probs = at(o + 3072, "probs", [P, 2, SW])
        gbias = at(o + 6144, "gbias", [P, NC])

        cw = take("cw", [P, KT, CONV_K + 1])
        cwk = take("cwk", [P, CONV_K + 1])
        ident = take("ident", [P, P])
        vec = take("vec", [P, V_N])
        rope_cs = take("rope_cs", [P, 2, TT, HALF])
        stat = take("stat", [P, 80])
        pos_i = take("pos_i", [P, TT], I32)
        assert cursor[0] <= nc.sbuf_usable_end, (cursor[0], nc.sbuf_usable_end)

        def st(n, w=TT):
            return stat[:, n:n + w]

        eps = st(0, 1)
        ss_x, sd_x, rs_x = st(2), st(4), st(6)
        ss_q, sd_q, rs_q = st(8), st(10), st(12)
        ss_kv, sd_kv, rs_kv = st(14), st(16), st(18)
        ss_part = stat[:, 20:28].rearrange("p (t c) -> p t c", t=TT)
        ss_sum, sd_n = st(28), st(30)
        rs_mem, rs_1, rs_2, rs_3 = st(32), st(34), st(36), st(38)
        top, ntop, den, rden = st(40, 4), st(44, 4), st(48, 4), st(52, 4)
        xtop, xntop, xden, xrden = st(56, 8), st(40, 8), st(64, 8), st(72, 8)

        ps = ctx.enter_context(nc.psum_tensor("ps", [P, 8, NC], F32))

        def sem(name):
            return ctx.enter_context(nc.semaphore(name))

        landed = [sem(f"landed{n}") for n in range(RING)]
        hi_ready = sem("hi_ready")
        lo_ready = sem("lo_ready")
        used = sem("used")
        chunk_out = sem("chunk_out")
        turned = sem("turned")
        turn_hi = sem("turn_hi")
        turn_lo = sem("turn_lo")
        x_landed, vec_landed, cw_landed, pos_landed = (sem(n) for n in ("x_landed", "vec_landed", "cw_landed", "pos_landed"))
        consts, mask_ready, mean_ready = sem("consts"), sem("mask_ready"), sem("mean_ready")
        vec_turned, vec_ready, cw_turned = (sem(n) for n in ("vec_turned", "vec_ready", "cw_turned"))
        angle_step, angle_ready, rope_ready = (sem(n) for n in ("angle_step", "angle_ready", "rope_ready"))
        ss_ready, sum_ready, sd_ready, rs_ready = (sem(n) for n in ("ss_ready", "sum_ready", "sd_ready", "rs_ready"))
        sg_ready = sem("sg_ready")
        conv_step = sem("conv_step")
        ln_added, ln_mean, ln_centred, ln_squared, ln_var = (sem(n) for n in ("ln_added", "ln_mean", "ln_centred", "ln_squared", "ln_var"))
        ln_root, ln_scaled, silu_done, st_hi, st_lo = (sem(n) for n in ("ln_root", "ln_scaled", "silu_done", "st_hi", "st_lo"))
        kpe_ready, kpe_prod, kpe_rotated, kpe_turned, kpeT_ready = (sem(n) for n in ("kpe_ready", "kpe_prod", "kpe_rotated", "kpe_turned", "kpeT_ready"))
        q_ready, kv_ready, q_prod, q_rotated = (sem(n) for n in ("q_ready", "kv_ready", "q_prod", "q_rotated"))
        qk_turned, qT_ready, kT_ready = (sem(n) for n in ("qk_turned", "qT_ready", "kT_ready"))
        scored, masked, ntop_ready = (sem(n) for n in ("scored", "masked", "ntop_ready"))
        exp_ready, rden_ready, probs_ready = (sem(n) for n in ("exp_ready", "rden_ready", "probs_ready"))
        p_turned, pT_ready = sem("p_turned"), sem("pT_ready")
        o_ready, o_hi, o_lo = (sem(n) for n in ("o_ready", "o_hi", "o_lo"))
        bias_landed, gate_ready = sem("bias_landed"), sem("gate_ready")
        mem_landed = [sem("mem_landed0"), sem("mem_landed1")]
        gated, res_landed = sem("gated"), sem("res_landed")
        x_scored, x_top, x_ntop, x_exp, x_rden, x_probs = (sem(n) for n in ("x_scored", "x_top", "x_ntop", "x_exp", "x_rden", "x_probs"))
        x_pturned, x_pT, x_o, x_ohi, x_olo = (sem(n) for n in ("x_pturned", "x_pT", "x_o", "x_ohi", "x_olo"))
        relu_ready, fin_landed, fin_ready, stored = (sem(n) for n in ("relu_ready", "fin_landed", "fin_ready", "stored"))

        block = ctx.enter_context(nc.Block())

        def wait(eng, s, value):
            if not isinstance(value, int) or value > 0:
                eng.wait_ge(s, value)

        @block.sync
        def _(sp):
            def load(u, r, src, kts=2, width=NC):
                wait(sp, lo_ready, u - RING + 1 + r)
                sp.dma_start(raw[:, u % RING, 0:kts * width].rearrange("p (k n) -> p k n", k=kts),
                             src).then_inc(landed[u % RING], 16)

            def load_chunk(u, r, w, col):
                for k in range(UPC):
                    load(u + k, r, w[:, 2 * k:2 * k + 2, ds(col, NC)])

            for t in range(TT):
                sp.dma_start(x_in[:, t, :], x_v[:, t, :]).then_inc(x_landed, 16)
            load_chunk(U_CONV, 0, w_in, COL_G)
            load_chunk(U_CONV + UPC, 0, w_in, COL_A)
            with sp.Fori(0, CH - 1) as i:
                load_chunk(U_CONV + 2 * UPC, i * (2 * UPC), w_in, i * NC + (COL_G + NC))
                load_chunk(U_CONV + 3 * UPC, i * (2 * UPC), w_in, i * NC + (COL_A + NC))
            load_chunk(U_LORA, 0, w_in, COL_CQ)
            load_chunk(U_LORA + UPC, 0, w_in, COL_CKV)
            load(U_KPE, 0, w_in[:, :, COL_KPE:COL_KPE + ROPE], KT, ROPE)

            with sp.Fori(0, PAIRS) as j:
                r = j * ATT_UNITS
                for n in range(2):
                    load(U_ATT + n, r, w_uq[:, 2 * n:2 * n + 2, ds(j * QW, QW)], 2, QW)
                for n in range(2):
                    load(U_ATT + 2 + n, r, w_ukv[:, 2 * n:2 * n + 2, ds(j * KVW, KVW)])
                load_chunk(U_ATT + 4, r, w_in, j * NC + COL_GATE)
                sp.wait_ge(turned, 2 * (T_CKV + 1))
                sp.wait_ge(chunk_out, j + N_GATE)
                sp.dma_start(gbias[:], b_gate[:, ds(j * NC, NC)].to_broadcast([P, NC])).then_inc(bias_landed, 16)

            for c in range(CH):
                load_chunk(U_MLA + UPC * c, 0, w_mla_out, NC * c)
            for c in range(2):
                load_chunk(U_XKV + UPC * c, 0, w_xkv, NC * c)
            for c in range(CH):
                load_chunk(U_COUT + UPC * c, 0, w_conv_out, NC * c)
            sp.wait_ge(st_lo, KT // 4)
            sp.dma_start(xres[:], x_v).then_inc(res_landed, 16)
            for c in range(CH):
                load_chunk(U_WOUT + UPC * c, 0, w_out, NC * c)
            load_chunk(U_XQ, 0, w_xq, 0)
            for c in range(CH):
                for n in range(2):
                    load(U_XO + 2 * c + n, 0, w_xo[:, 2 * n:2 * n + 2, NC * c:NC * (c + 1)])
            with sp.Fori(0, GROUPS) as g:
                r = g * FF_UNITS
                for c in range(CH):
                    load_chunk(U_FF + UPC * c, r, w_ff1, g * D + NC * c)
                for c in range(CH):
                    for k in range(UPC):
                        load(U_FF + UPC * (CH + c) + k, r, w_ff2[:, ds(g * KT + 2 * k, 2), NC * c:NC * (c + 1)])
            for c in range(CH):
                sp.wait_ge(fin_ready, c + 1)
                sp.dma_start(out_v[:, :, NC * c:NC * (c + 1)], fin[:, :, NC * c:NC * (c + 1)]).then_inc(stored, 16)
            sp.wait_ge(stored, 16 * CH)

        @block.gpsimd
        def _(pool):
            def vector_rows(v):
                return v.rearrange("o (k p) -> (o k) p", p=P)

            for n, v in enumerate((norm_mix_g, conv_ln_g, conv_ln_b, norm_mem_g, mem_norm_g, norm_ffn_g)):
                pool.dma_start(vec_rows[KT * n:KT * (n + 1), :], vector_rows(v)).then_inc(vec_landed, 16)
            pool.dma_start(vec_rows[V_QG:V_QG + LT, :], vector_rows(q_norm_g)).then_inc(vec_landed, 16)
            pool.dma_start(vec_rows[V_KG:V_KG + LT, :], vector_rows(kv_norm_g)).then_inc(vec_landed, 16)
            pool.memset(ident[:], 0.0).then_inc(consts, 1)
            pool.wait_ge(consts, 1)
            pool.affine_select(out=ident[:], in_=ident[:], compare_op=ALU.not_equal, fill=1.0, base=0,
                               pattern=[[-1, P]], channel_multiplier=1).then_inc(consts, 1)
            pool.memset(eps, EPS).then_inc(consts, 1)
            pool.dma_start(cw_rows[0:CONV_K, :], conv_w.rearrange("o k n -> (o k) n")).then_inc(cw_landed, 16)
            pool.dma_start(cw_rows[CONV_K:CONV_K + 1, :], conv_b).then_inc(cw_landed, 16)
            pool.dma_start(pos_i[:], positions.rearrange("o (t p) -> p (o t)", p=P), allow_slow_non_contiguous=True).then_inc(pos_landed, 16)
            pool.memset(hconv[:, :, 0:PAD], 0.0).then_inc(consts, 1)
            pool.memset(mask[:], 0.0).then_inc(mask_ready, 1)
            pool.wait_ge(mask_ready, 1)
            pool.memset(mask[0:64, 64:128], NEG).then_inc(mask_ready, 1)
            pool.memset(mask[0:64, SW - 64:SW], NEG).then_inc(mask_ready, 1)

            ang, hi_p, lo_p, prod, rnd, total = (rope_tmp[:, n, :] for n in range(6))
            steps = [0]

            def step(ins):
                steps[0] += 1
                ins.then_inc(angle_step, 1)
                pool.wait_ge(angle_step, steps[0])

            for n, f in enumerate(inv_freqs()):
                step(pool.memset(ang.rearrange("p (t f) -> p t f", t=TT)[:, :, n:n + 1], f))
            pool.wait_ge(pos_landed, 16)
            step(pool.tensor_copy(hi_p[:, 0:TT], pos_i[:]))
            for t in range(TT):
                half = ang[:, t * HALF:(t + 1) * HALF]
                step(pool.tensor_scalar(half, half, hi_p[:, t:t + 1], None, ALU.mult))
            step(pool.tensor_scalar(hi_p, ang, 4097.0, None, ALU.mult))
            step(pool.tensor_tensor(lo_p, hi_p, ang, ALU.subtract))
            step(pool.tensor_tensor(hi_p, hi_p, lo_p, ALU.subtract))
            step(pool.tensor_tensor(lo_p, ang, hi_p, ALU.subtract))
            step(pool.memset(total, 0.0))
            for part in (hi_p, lo_p):
                for n, piece in enumerate(turn_pieces(5)):
                    step(pool.tensor_scalar(prod, part, piece, None, ALU.mult))
                    for _ in range(2 if n == 0 else 1):
                        step(pool.tensor_scalar(rnd, prod, MAGIC, None, ALU.add))
                        step(pool.tensor_scalar(rnd, rnd, MAGIC, None, ALU.subtract))
                        step(pool.tensor_tensor(prod, prod, rnd, ALU.subtract))
                    step(pool.tensor_tensor(total, total, prod, ALU.add))
            step(pool.tensor_scalar(prod, total, 0.25, None, ALU.add))
            for n, angle in enumerate((prod, total)):
                step(pool.tensor_scalar(rnd, angle, MAGIC, None, ALU.add))
                step(pool.tensor_scalar(rnd, rnd, MAGIC, None, ALU.subtract))
                pool.tensor_tensor(rope_cs[:, n, :, :].rearrange("p t f -> p (t f)"), angle, rnd, ALU.subtract).then_inc(angle_ready, 1)
                pool.wait_ge(angle_ready, n + 1)

            def products(x1, x2, h, s):
                for n, (v, c) in enumerate(((x1, 0), (x2, 1), (x2, 0), (x1, 1))):
                    pool.tensor_tensor(rot[:, n, h, :, :], v, rope_cs[:, c, :, :], ALU.mult).then_inc(s, 1)

            def sums(x1, x2, h, s):
                pool.tensor_tensor(x1, rot[:, 0, h, :, :], rot[:, 1, h, :, :], ALU.subtract).then_inc(s, 1)
                pool.tensor_tensor(x2, rot[:, 2, h, :, :], rot[:, 3, h, :, :], ALU.add).then_inc(s, 1)

            pool.wait_ge(rope_ready, 1)
            pool.wait_ge(kpe_ready, 1)
            products(kpe_row[:, :, 0:HALF], kpe_row[:, :, HALF:ROPE], 0, kpe_prod)
            pool.wait_ge(kpe_prod, 4)
            sums(kpe_rot[:, :, 0:HALF], kpe_rot[:, :, HALF:ROPE], 0, kpe_rotated)
            pool.wait_ge(kpe_rotated, 2)

            with pool.Fori(0, PAIRS) as j:
                pool.wait_ge(q_ready, j + 1)
                pe_cols = [h * (NOPE + ROPE) + NOPE for h in range(2)]
                for h, a in enumerate(pe_cols):
                    products(q_row[:, :, a:a + HALF], q_row[:, :, a + HALF:a + ROPE], h, q_prod)
                pool.wait_ge(q_prod, j * 8 + 8)
                for h, a in enumerate(pe_cols):
                    sums(q_row[:, :, a:a + HALF], q_row[:, :, a + HALF:a + ROPE], h, q_rotated)
                pool.wait_ge(q_rotated, j * 4 + 4)

            pool.wait_ge(o_ready, PAIRS)
            pool.wait_ge(chunk_out, N_MLA)
            for c in range(CH):
                if c >= 2:
                    pool.wait_ge(turned, 2 * (T_MEM + c - 1))
                    pool.wait_ge(ss_ready, SS_KV + TT * (c - 1))
                pool.dma_start(rows[:, c % 2, :, :], mem_v[:, :, NC * c:NC * (c + 1)]).then_inc(mem_landed[c % 2], 16)
            pool.wait_ge(conv_step, KT * CONV_STEPS + 1)
            pool.memset(mean_w[:], 1.0 / D).then_inc(mean_ready, 1)
            pool.wait_ge(chunk_out, N_WOUT)
            pool.dma_start(fin_g[:], final_norm_g.rearrange("(o n) -> o n", o=1).to_broadcast([P, D])).then_inc(fin_landed, 16)

        @block.scalar
        def _(act):
            def hi(u, r=0):
                s = u % RING
                act.wait_ge(landed[s], 16 * (u // RING + 1) + r * (16 // RING))
                wait(act, used, u - RING + 1 + r)
                act.activation(whi[:, s, :], raw[:, s, :], ACT.Copy).then_inc(hi_ready, 1)

            def turn_out(turn, dst, k0, gain=None):
                for b in range(2):
                    act.wait_ge(turned, turn * 2 + (b + 1))
                    if gain is None:
                        last = act.activation(dst[:, ds(k0 + 2 * b, 2), :], bank_blocks(b), ACT.Copy)
                    else:
                        for k in (2 * b, 2 * b + 1):
                            last = act.activation(dst[:, k0 + k, :], ps[:, 6 + b, SEQ * (k % 2):SEQ * (k % 2 + 1)], ACT.Copy,
                                                  scale=vec[:, gain + k0 + k:gain + k0 + k + 1])
                    last.then_inc(turn_hi, 1)

            def bank_blocks(b):
                return ps[:, 6 + b, :].rearrange("p (k s) -> p k s", k=2)

            def square_sums(scratch, src, to):
                for t in range(TT):
                    act.activation(scratch[:, t, :], src[:, t, :], ACT.Square, accum_out=to[:, t:t + 1]).then_inc(ss_ready, 1)

            def chunk_squares(scratch, src, c, done):
                act.wait_ge(ss_ready, done)
                for t in range(TT):
                    act.activation(scratch[:, t, :], src[:, t, :], ACT.Square, accum_out=ss_part[:, t, c:c + 1]).then_inc(ss_ready, 1)

            def root(dst, src, width):
                act.activation(dst, src, ACT.Sqrt, bias=eps, scale=1.0 / width).then_inc(sd_ready, 1)

            def glu_gate():
                for t in range(TT):
                    last = act.activation(rows[:, 1, t, :], ps[:, 2 + t, :], ACT.Sigmoid, scale=rs_x[:, t:t + 1])
                last.then_inc(sg_ready, 1)

            def scaled_rows(dst, bank, width, scale, done):
                for t in range(TT):
                    last = act.activation(dst[:, t, :], ps[:, bank + t, 0:width], ACT.Copy, scale=scale[:, t:t + 1])
                last.then_inc(done, 1)

            act.wait_ge(consts, 3)
            act.wait_ge(vec_ready, 1)
            turn_out(T_X, a_hi, 0, V_MIX)
            hi(0)
            hi(1)
            turn_out(T_X + 1, a_hi, 4, V_MIX)
            hi(2)
            hi(3)
            hi(4)
            turn_out(T_X + 2, a_hi, 8, V_MIX)
            hi(5)
            hi(6)
            turn_out(T_X + 3, a_hi, 12, V_MIX)
            hi(7)
            square_sums(sq_x, x_in, ss_x)
            hi(8)
            act.wait_ge(ss_ready, SS_X)
            root(sd_x, ss_x, D)
            for k in range(6, 2 * UPC):
                hi(U_CONV + k + LEAD)
                if k == 9:
                    act.wait_ge(used, U_CONV + UPC)
                    act.wait_ge(rs_ready, R_X)
                    glu_gate()
                if k == 12:
                    act.wait_ge(angle_ready, 2)
                    cs = rope_cs[:].rearrange("p c t f -> p (c t f)")
                    act.activation(cs, cs, ACT.Sin, scale=TWO_PI).then_inc(rope_ready, 1)
            act.wait_ge(consts, 4)
            with act.Fori(1, CH) as i:
                r = i * (2 * UPC)
                for k in range(2 * UPC):
                    hi(U_CONV + k + LEAD, r)
                    if k == 2:
                        turn_out(i + (T_CONV - 1), hconv[:, :, PAD:], i * 4 - 4)
                    if k == 8:
                        act.wait_ge(used, r + (U_CONV + UPC))
                        act.wait_ge(chunk_out, i)
                        glu_gate()

            for k in range(UPC):
                hi(U_LORA + k + LEAD)
                if k == 2:
                    turn_out(T_CONV + CH - 1, hconv[:, :, PAD:], 4 * (CH - 1))
            act.wait_ge(used, U_LORA + UPC)
            scaled_rows(rows[:, 0, :, :], 2, LORA, rs_x, chunk_out)
            act.wait_ge(chunk_out, N_CQ + 1)
            square_sums(sq_lat, rows[:, 0, :, :], ss_q)
            act.wait_ge(ss_ready, SS_Q)
            root(sd_q, ss_q, LORA)
            for k in range(UPC):
                hi(U_LORA + UPC + k + LEAD)
                if k == 2:
                    turn_out(T_CQ, cq_hi, 0, V_QG)
            act.wait_ge(used, U_LORA + 2 * UPC)
            scaled_rows(rows[:, 1, :, :], 0, LORA, rs_x, chunk_out)
            act.wait_ge(chunk_out, N_CKV + 1)
            act.wait_ge(ss_ready, SS_Q)
            square_sums(sq_lat, rows[:, 1, :, :], ss_kv)
            act.wait_ge(ss_ready, SS_KV)
            root(sd_kv, ss_kv, LORA)
            hi(U_KPE + LEAD)
            act.wait_ge(used, U_KPE + 1)
            scaled_rows(kpe_row, 4, ROPE, rs_x, kpe_ready)
            turn_out(T_CKV, ckv_hi, 0, V_KG)
            act.wait_ge(kpe_turned, 1)
            act.activation(kpeT[:], ps[0:ROPE, 5, 0:SEQ], ACT.Copy).then_inc(kpeT_ready, 1)

            with act.Fori(0, PAIRS) as j:
                r = j * ATT_UNITS
                for k in range(ATT_UNITS):
                    hi(U_ATT + k + LEAD, r)
                    if k == 3:
                        act.wait_ge(used, r + (U_ATT + 4))
                        act.wait_ge(rs_ready, R_KV)
                        scaled_rows(q_row, 2, QW, rs_q, q_ready)
                        scaled_rows(kv_row, 4, KVW, rs_kv, kv_ready)
                    if k == 5:
                        act.wait_ge(qk_turned, j * 3 + 1)
                        act.activation(qT[:].rearrange("p h s -> p (h s)"), ps[:, 6, :], ACT.Copy).then_inc(qT_ready, 1)
                        act.wait_ge(qk_turned, j * 3 + 2)
                        act.activation(kT[:].rearrange("p h s -> p (h s)"), ps[:, 7, :], ACT.Copy).then_inc(kT_ready, 1)
                        act.wait_ge(qk_turned, j * 3 + 3)
                        act.activation(qrT[:].rearrange("p h s -> p (h s)"), ps[0:ROPE, 2, :], ACT.Copy).then_inc(qT_ready, 1)
                    if k == 7:
                        act.wait_ge(ntop_ready, j + 1)
                        for n, (h, a, b) in enumerate(SCORES):
                            act.activation(probs[:, h, a:b], probs[:, h, a:b], ACT.Exp, bias=ntop[:, n:n + 1], scale=SM,
                                           accum_out=den[:, n:n + 1]).then_inc(exp_ready, 1)
                    if k == 9:
                        act.wait_ge(p_turned, j * 2 + 1)
                        act.activation(pT[:, 0, :], ps[:, 5, 0:SW], ACT.Copy).then_inc(pT_ready, 1)
                        act.wait_ge(p_turned, j * 2 + 2)
                        act.activation(pT[:, 1, :], ps[:, 6, 0:SW], ACT.Copy).then_inc(pT_ready, 1)
                    if k == 10:
                        act.wait_ge(o_ready, j + 1)
                        act.activation(c_hi[:, ds(j * 2, 2), :], ps[:, 7, :].rearrange("p (k s) -> p k s", k=2), ACT.Copy).then_inc(o_hi, 1)

            for c in range(CH):
                for k in range(UPC):
                    hi(U_MLA + UPC * c + k + LEAD)
                    if k == 2:
                        act.wait_ge(mem_landed[c % 2], 16 * (c // 2 + 1))
                        chunk_squares(sq_mem, rows[:, c % 2, :, :], c, SS_KV + TT * c)
                        turn_out(T_MEM + c, m_hi, 4 * c, V_MEMN)
                    if k == 4:
                        act.wait_ge(chunk_out, N_MLA)
                        for half in (D, 0):
                            g = gates[:, :, half + NC * c:half + NC * (c + 1)]
                            act.activation(g, g, ACT.Sigmoid).then_inc(gate_ready, 1)
            act.wait_ge(sum_ready, 1)
            root(sd_n, ss_sum, D)

            for k in range(UPC):
                hi(U_XKV + k + LEAD)
                for m in ((0, 1), (2,), (3,))[k] if k < 3 else ():
                    act.wait_ge(ln_centred, m + 1)
                    act.activation(ln_sq[:, 4 * m:4 * m + 4, :], hconv[:, 4 * m:4 * m + 4, PAD:], ACT.Square).then_inc(ln_squared, 1)
                if k == 7:
                    act.wait_ge(ln_var, 1)
                    act.activation(acc[:, 0, :], ps[:, 5, 0:SEQ], ACT.Sqrt, bias=eps).then_inc(ln_root, 1)
            act.wait_ge(used, U_XKV + UPC)
            act.wait_ge(chunk_out, N_XK)
            act.wait_ge(rs_ready, R_MEM)
            scaled_rows(rows[:, pair_of(N_XK), :, :], 2 * pair_of(N_XK), NC, rs_mem, chunk_out)
            for k in range(UPC):
                hi(U_XKV + UPC + k + LEAD)
                if 1 <= k < 5:
                    m = k - 1
                    act.wait_ge(ln_scaled, m + 1)
                    for n in range(4 * m, 4 * m + 4):
                        act.activation(hconv[:, n, PAD:], hconv[:, n, PAD:], ACT.Silu, bias=vec[:, V_LB + n:V_LB + n + 1],
                                       scale=vec[:, V_LG + n:V_LG + n + 1]).then_inc(silu_done, 1)
                if 2 <= k < 6:
                    m = k - 2
                    act.wait_ge(silu_done, 4 * m + 4)
                    act.activation(a_hi[:, 4 * m:4 * m + 4, :], hconv[:, 4 * m:4 * m + 4, PAD:], ACT.Copy).then_inc(st_hi, 1)
            act.wait_ge(used, U_XKV + 2 * UPC)
            scaled_rows(xv, 2 * pair_of(N_XV), NC, rs_mem, chunk_out)

            for c in range(CH):
                for k in range(UPC):
                    hi(U_COUT + UPC * c + k + LEAD)
                    if k == 3 and c == 0:
                        turn_out(T_XK, xkT, 0)
                    if k == 3 and c:
                        turn_out(T_MRG + c - 1, c_hi, 4 * (c - 1))
            for c in range(CH):
                for k in range(UPC):
                    hi(U_WOUT + UPC * c + k + LEAD)
                    if k == 3 and c == 0:
                        turn_out(T_MRG + CH - 1, c_hi, 4 * (CH - 1))
                    if k == 3 and c:
                        turn_out(T_X1 + c - 1, a_hi, 4 * (c - 1), V_NMEM)
                act.wait_ge(chunk_out, N_WOUT + c + 1)
                chunk_squares(sq_res, xres[:, :, NC * c:NC * (c + 1)], c, SS_MEM + TT * c)
            for k in range(UPC):
                hi(U_XQ + k + LEAD)
                if k == 3:
                    turn_out(T_X1 + CH - 1, a_hi, 4 * (CH - 1), V_NMEM)
                    act.wait_ge(sum_ready, 2)
                    root(sd_n, ss_sum, D)
            act.wait_ge(used, U_XQ + UPC)
            act.wait_ge(rs_ready, R_1)
            act.wait_ge(chunk_out, N_XQ)
            scaled_rows(rows[:, pair_of(N_XQ), :, :], 2 * pair_of(N_XQ), NC, rs_1, chunk_out)
            turn_out(T_XQ, xqT, 0)
            for h in range(XH):
                act.wait_ge(x_ntop, h + 1)
                for t in range(TT):
                    n = TT * h + t
                    act.activation(xp[:, h, t, :], ps[:, h, SEQ * t:SEQ * (t + 1)], ACT.Exp, bias=xntop[:, n:n + 1], scale=XSM,
                                   accum_out=xden[:, n:n + 1]).then_inc(x_exp, 1)
            for h in range(XH):
                act.wait_ge(x_pturned, h + 1)
                act.activation(xpT[:, h, :, :], ps[:, 4 + h, :].rearrange("p (k s) -> p k s", k=2), ACT.Copy).then_inc(x_pT, 1)
            for b in range(2):
                act.wait_ge(x_o, b + 1)
                act.activation(xo_hi[:, 2 * b:2 * b + 2, :], ps[:, b, :].rearrange("p (k s) -> p k s", k=2), ACT.Copy).then_inc(x_ohi, 1)
            for c in range(CH):
                for k in range(2):
                    hi(U_XO + 2 * c + k + LEAD)
                if c:
                    turn_out(T_X2 + c - 1, a_hi, 4 * (c - 1), V_FFN)
                act.wait_ge(chunk_out, N_XO + c + 1)
                chunk_squares(sq_res, xres[:, :, NC * c:NC * (c + 1)], c, SS_1 + TT * c)
            turn_out(T_X2 + CH - 1, a_hi, 4 * (CH - 1), V_FFN)
            act.wait_ge(sum_ready, 3)
            root(sd_n, ss_sum, D)

            def ff_group(g, r, last):
                for c in range(CH):
                    for k in range(UPC):
                        hi(U_FF + UPC * c + k + LEAD, r)
                        if k == 3 and c:
                            turn_out(g * CH + (T_FF + c - 1), c_hi, 4 * (c - 1))
                    act.wait_ge(used, r + (U_FF + UPC * (c + 1)))
                    act.wait_ge(rs_ready, R_2)
                    scaled_relu(c)
                for c in range(CH):
                    for k in range(UPC):
                        if not last or UPC * (CH + c) + k + LEAD < FF_UNITS:
                            hi(U_FF + UPC * (CH + c) + k + LEAD, r)
                        if k == 3 and c == 0:
                            turn_out(g * CH + (T_FF + CH - 1), c_hi, 4 * (CH - 1))
                    if last:
                        act.wait_ge(chunk_out, N_FF + g * 2 * CH + CH + c + 1)
                        chunk_squares(sq_res, xres[:, :, NC * c:NC * (c + 1)], c, SS_2 + TT * c)

            def scaled_relu(c):
                p = pair_of(N_FF + c)
                for t in range(TT):
                    last = act.activation(rows[:, p, t, :], ps[:, 2 * p + t, :], ACT.Relu, scale=rs_2[:, t:t + 1])
                last.then_inc(relu_ready, 1)

            with act.Fori(0, GROUPS - 1) as g:
                ff_group(g, g * FF_UNITS, False)
            ff_group(GROUPS - 1, (GROUPS - 1) * FF_UNITS, True)
            act.wait_ge(sum_ready, 4)
            root(sd_n, ss_sum, D)

        @block.vector
        def _(dve):
            def lo(u, r=0):
                s = u % RING
                dve.wait_ge(hi_ready, u + 1 + r)
                dve.tensor_tensor(wlo[:, s, :], raw[:, s, :], whi[:, s, :].bitcast(F32), ALU.subtract).then_inc(lo_ready, 1)

            def bank_blocks(b):
                return ps[:, 6 + b, :].rearrange("p (k s) -> p k s", k=2)

            def turn_low(turn, dst_lo, dst_hi, k0, gain=None):
                for b in range(2):
                    dve.wait_ge(turn_hi, turn * 2 + (b + 1))
                    if gain is None:
                        last = dve.tensor_tensor(dst_lo[:, k0 + 2 * b:k0 + 2 * b + 2, :], bank_blocks(b),
                                                 dst_hi[:, k0 + 2 * b:k0 + 2 * b + 2, :].bitcast(F32), ALU.subtract)
                    else:
                        for k in (2 * b, 2 * b + 1):
                            g = gain + k0 + k
                            last = dve.scalar_tensor_tensor(out=dst_lo[:, k0 + k, :], in0=ps[:, 6 + b, SEQ * (k % 2):SEQ * (k % 2 + 1)],
                                                            scalar=vec[:, g:g + 1], in1=dst_hi[:, k0 + k, :].bitcast(F32),
                                                            op0=ALU.mult, op1=ALU.subtract)
                    last.then_inc(turn_lo, 1)

            def reciprocal(dst, src, n):
                dve.wait_ge(sd_ready, n)
                dve.reciprocal(dst, src).then_inc(rs_ready, 1)

            def add_parts(squares, n):
                dve.wait_ge(ss_ready, squares)
                dve.tensor_reduce(ss_sum, ss_part, AX_X, ALU.add).then_inc(sum_ready, 1)

            def glu():
                for t in range(TT):
                    last = dve.scalar_tensor_tensor(out=rows[:, 0, t, :], in0=ps[:, t, :], scalar=rs_x[:, t:t + 1],
                                                    in1=rows[:, 1, t, :], op0=ALU.mult, op1=ALU.mult)
                last.then_inc(chunk_out, 1)

            def conv(kt, steps):
                for n in steps:
                    h = hconv[:, ds(kt, 1), :].rearrange("p k s -> p (k s)")
                    tap = n - 1
                    in_turn = n in (0, 1, CONV_STEPS - 1)
                    dve.wait_ge(conv_step, kt * CONV_STEPS + (n + 1 if in_turn else n))
                    to = acc[:, tap % 2, :]
                    if n == 0:
                        ins = dve.tensor_copy(cwk[:], cw[:, ds(kt, 1), :].rearrange("p k s -> p (k s)"))
                    elif n == CONV_STEPS - 1:
                        ins = dve.tensor_tensor(h[:, PAD:HC], acc[:, 0, :], acc[:, 1, :], ALU.add)
                    elif tap == 0:
                        ins = dve.tensor_scalar(to, h[:, 0:SEQ], cwk[:, 0:1], cwk[:, CONV_K:CONV_K + 1], ALU.mult, ALU.add)
                    elif tap == 1:
                        ins = dve.tensor_scalar(to, h[:, 1:1 + SEQ], cwk[:, 1:2], None, ALU.mult)
                    else:
                        ins = dve.scalar_tensor_tensor(out=to, in0=h[:, tap:tap + SEQ], scalar=cwk[:, tap:tap + 1], in1=to,
                                                       op0=ALU.mult, op1=ALU.add)
                    ins.then_inc(conv_step, 1)

            def share(k, parts):
                return range(CONV_STEPS * k // parts, CONV_STEPS * (k + 1) // parts)

            dve.wait_ge(vec_turned, 1)
            dve.tensor_copy(vec[:], ps[:, 5, 0:V_N]).then_inc(vec_ready, 1)
            dve.wait_ge(vec_ready, 1)
            turn_low(T_X, a_lo, a_hi, 0, V_MIX)
            lo(0)
            lo(1)
            turn_low(T_X + 1, a_lo, a_hi, 4, V_MIX)
            lo(2)
            lo(3)
            lo(4)
            turn_low(T_X + 2, a_lo, a_hi, 8, V_MIX)
            lo(5)
            lo(6)
            turn_low(T_X + 3, a_lo, a_hi, 12, V_MIX)
            lo(7)
            lo(8)
            for k in range(6, 2 * UPC):
                lo(U_CONV + k + LEAD)
                if k == 8:
                    reciprocal(rs_x, sd_x, R_X)
                if k == 10:
                    dve.wait_ge(cw_turned, 1)
                    dve.tensor_copy(cw[:].rearrange("p k s -> p (k s)"), ps[:, 4, :]).then_inc(conv_step, 1)
            dve.wait_ge(used, U_CONV + 2 * UPC)
            dve.wait_ge(sg_ready, 1)
            dve.wait_ge(rs_ready, R_X)
            glu()
            with dve.Fori(1, CH) as i:
                r = i * (2 * UPC)
                for k in range(2 * UPC):
                    lo(U_CONV + k + LEAD, r)
                    if k == 4:
                        dve.wait_ge(turn_hi, i * 2 + 2 * T_CONV)
                    if 4 <= k < 15:
                        conv(i - 1, share(k - 4, 11))
                dve.wait_ge(used, r + (U_CONV + 2 * UPC))
                dve.wait_ge(sg_ready, i + 1)
                glu()

            for k in range(UPC):
                lo(U_LORA + k + LEAD)
                conv(CH - 1, share(k, UPC))
            reciprocal(rs_q, sd_q, R_Q)
            dve.wait_ge(turn_hi, 2 * (T_CONV + 2))
            for k in range(UPC):
                lo(U_LORA + UPC + k + LEAD)
                if k == 2:
                    turn_low(T_CQ, cq_lo, cq_hi, 0, V_QG)
                conv(CH, share(k, UPC))
            reciprocal(rs_kv, sd_kv, R_KV)
            lo(U_KPE + LEAD)
            turn_low(T_CKV, ckv_lo, ckv_hi, 0, V_KG)

            dve.wait_ge(mask_ready, 3)
            dve.wait_ge(turn_hi, 2 * (T_CONV + CH))
            CONV_AT = (0, 1, 2, 4, 5, 6, 7, 8, 9, 10)
            with dve.Fori(0, PAIRS) as j:
                r = j * ATT_UNITS
                for k in range(ATT_UNITS):
                    lo(U_ATT + k + LEAD, r)
                    if k == 6:
                        dve.wait_ge(scored, j * 2 + 2)
                        conv(j + (CH + 1), share(CONV_AT.index(k), len(CONV_AT)))
                        for n, (h, a, b) in enumerate(SCORES):
                            dve.tensor_tensor_reduce(probs[:, h, a:b], ps[:, 3 + h, a:b], mask[:, a:b], 1.0, NEG, ALU.add, ALU.max,
                                                     top[:, n:n + 1]).then_inc(masked, 1)
                        dve.wait_ge(masked, j * 4 + 4)
                        dve.tensor_scalar(ntop, top, -SM, None, ALU.mult).then_inc(ntop_ready, 1)
                    if k == 8:
                        dve.wait_ge(exp_ready, j * 4 + 4)
                        dve.reciprocal(rden, den).then_inc(rden_ready, 1)
                        dve.wait_ge(rden_ready, j + 1)
                        for n, (h, a, b) in enumerate(SCORES):
                            dve.tensor_scalar(probs[:, h, a:b], probs[:, h, a:b], rden[:, n:n + 1], None, ALU.mult).then_inc(probs_ready, 1)
                    if k == 10:
                        dve.wait_ge(o_hi, j + 1)
                        dve.tensor_tensor(c_lo[:, ds(j * 2, 2), :], ps[:, 7, :].rearrange("p (k s) -> p k s", k=2),
                                          c_hi[:, ds(j * 2, 2), :].bitcast(F32), ALU.subtract).then_inc(o_lo, 1)
                    if k in CONV_AT and k != 6:
                        conv(j + (CH + 1), share(CONV_AT.index(k), len(CONV_AT)))
                dve.wait_ge(used, r + (U_ATT + ATT_UNITS))
                dve.wait_ge(bias_landed, j * 16 + 16)
                for t in range(TT):
                    last = dve.scalar_tensor_tensor(out=gates[:, t, ds(j * NC, NC)], in0=ps[:, t, :], scalar=rs_x[:, t:t + 1],
                                                    in1=gbias[:], op0=ALU.mult, op1=ALU.add)
                last.then_inc(chunk_out, 1)

            def ln_tree(src, first):
                adds = ((ln_sum[:, 0:4, :], src[:, 0:4, :], src[:, 8:12, :]), (ln_sum[:, 4:8, :], src[:, 4:8, :], src[:, 12:16, :]),
                        (ln_sum[:, 0:4, :], ln_sum[:, 0:4, :], ln_sum[:, 4:8, :]),
                        (ln_sum[:, 0:2, :], ln_sum[:, 0:2, :], ln_sum[:, 2:4, :]),
                        (ln_sum[:, 0:1, :], ln_sum[:, 0:1, :], ln_sum[:, 1:2, :]))
                return adds

            def ln_add(src, first, n):
                to, a, b = ln_tree(src, first)[n]
                if n >= 2:
                    dve.wait_ge(ln_added, first + n)
                dve.tensor_tensor(to, a, b, ALU.add).then_inc(ln_added, 1)

            def spread(v):
                return v.rearrange("p (k s) -> p k s", k=1).to_broadcast([P, 4, SEQ])

            def centre(m):
                dve.wait_ge(ln_mean, 1)
                dve.tensor_tensor(y[:, 4 * m:4 * m + 4, :], y[:, 4 * m:4 * m + 4, :], spread(ps[:, 4, 0:SEQ]), ALU.subtract).then_inc(ln_centred, 1)

            y = hconv[:, :, PAD:]
            for c in range(CH):
                for k in range(UPC):
                    lo(U_MLA + UPC * c + k + LEAD)
                    if k == 2:
                        turn_low(T_MEM + c, m_lo, m_hi, 4 * c, V_MEMN)
                    if c < CH - 1:
                        conv(CH + 1 + PAIRS + c, share(k, UPC))
                    elif k < 5:
                        if k == 0:
                            dve.wait_ge(conv_step, KT * CONV_STEPS + 1)
                        ln_add(y, 0, k)
                    elif k == 5:
                        add_parts(SS_MEM, 1)
                    else:
                        centre(k - 6)
                n = N_MLA + c
                dve.wait_ge(used, U_MLA + UPC * (c + 1))
                dve.wait_ge(gate_ready, 2 * c + 1)
                g = gates[:, :, D + NC * c:D + NC * (c + 1)]
                dve.tensor_tensor(g, ps[:, 2 * pair_of(n):2 * pair_of(n) + 2, :], g, ALU.mult).then_inc(chunk_out, 1)

            for k in range(UPC):
                lo(U_XKV + k + LEAD)
                if k < 2:
                    centre(k + 2)
                if k == 1:
                    reciprocal(rs_mem, sd_n, R_MEM)
                if k in (2, 3):
                    dve.wait_ge(ln_squared, k + 1)
                    ln_add(ln_sq, 5, k - 2)
                if k == 4:
                    for n in (2, 3, 4):
                        ln_add(ln_sq, 5, n)
            for k in range(UPC):
                lo(U_XKV + UPC + k + LEAD)
                if k == 0:
                    dve.wait_ge(ln_root, 1)
                    dve.reciprocal(acc[:, 0, :], acc[:, 0, :]).then_inc(ln_root, 1)
                    dve.wait_ge(ln_root, 2)
                if k < 4:
                    dve.tensor_tensor(y[:, 4 * k:4 * k + 4, :], y[:, 4 * k:4 * k + 4, :], spread(acc[:, 0, :]), ALU.mult).then_inc(ln_scaled, 1)
                if 3 <= k < 7:
                    m = k - 3
                    dve.wait_ge(st_hi, m + 1)
                    dve.tensor_tensor(a_lo[:, 4 * m:4 * m + 4, :], y[:, 4 * m:4 * m + 4, :], a_hi[:, 4 * m:4 * m + 4, :].bitcast(F32),
                                      ALU.subtract).then_inc(st_lo, 1)

            for c in range(CH):
                for k in range(UPC):
                    lo(U_COUT + UPC * c + k + LEAD)
                    if k == 3 and c:
                        turn_low(T_MRG + c - 1, c_lo, c_hi, 4 * (c - 1))
                n = N_COUT + c
                p = pair_of(n)
                dve.wait_ge(used, U_COUT + UPC * (c + 1))
                dve.wait_ge(chunk_out, n)
                cols = slice(NC * c, NC * (c + 1))
                dve.tensor_tensor(rows[:, p, :, :], ps[:, 2 * p:2 * p + 2, :], gates[:, :, cols], ALU.mult).then_inc(gated, 1)
                dve.wait_ge(gated, c + 1)
                dve.tensor_tensor(rows[:, p, :, :], rows[:, p, :, :], gates[:, :, D + NC * c:D + NC * (c + 1)], ALU.add).then_inc(chunk_out, 1)

            def add_to_residual(n, c):
                p = pair_of(n)
                cols = xres[:, :, NC * c:NC * (c + 1)]
                dve.tensor_tensor(cols, ps[:, 2 * p:2 * p + 2, :], cols, ALU.add).then_inc(chunk_out, 1)

            for c in range(CH):
                for k in range(UPC):
                    lo(U_WOUT + UPC * c + k + LEAD)
                    if k == 3 and c == 0:
                        turn_low(T_MRG + CH - 1, c_lo, c_hi, 4 * (CH - 1))
                    if k == 3 and c:
                        turn_low(T_X1 + c - 1, a_lo, a_hi, 4 * (c - 1), V_NMEM)
                dve.wait_ge(used, U_WOUT + UPC * (c + 1))
                dve.wait_ge(res_landed, 16)
                add_to_residual(N_WOUT + c, c)
            for k in range(UPC):
                lo(U_XQ + k + LEAD)
                if k == 1:
                    add_parts(SS_1, 2)
                if k == 3:
                    turn_low(T_X1 + CH - 1, a_lo, a_hi, 4 * (CH - 1), V_NMEM)
                if k == 5:
                    reciprocal(rs_1, sd_n, R_1)
            for h in range(XH):
                dve.wait_ge(x_scored, h + 1)
                dve.tensor_reduce(xtop[:, TT * h:TT * (h + 1)], ps[:, h, :].rearrange("p (t m) -> p t m", t=TT), AX_X, ALU.max).then_inc(x_top, 1)
                dve.wait_ge(x_top, h + 1)
                dve.tensor_scalar(xntop[:, TT * h:TT * (h + 1)], xtop[:, TT * h:TT * (h + 1)], -XSM, None, ALU.mult).then_inc(x_ntop, 1)
            for h in range(XH):
                dve.wait_ge(x_exp, TT * (h + 1))
                dve.reciprocal(xrden[:, TT * h:TT * (h + 1)], xden[:, TT * h:TT * (h + 1)]).then_inc(x_rden, 1)
                dve.wait_ge(x_rden, h + 1)
                for t in range(TT):
                    n = TT * h + t
                    dve.tensor_scalar(xp[:, h, t, :], xp[:, h, t, :], xrden[:, n:n + 1], None, ALU.mult).then_inc(x_probs, 1)
            for b in range(2):
                dve.wait_ge(x_ohi, b + 1)
                dve.tensor_tensor(xo_lo[:, 2 * b:2 * b + 2, :], ps[:, b, :].rearrange("p (k s) -> p k s", k=2),
                                  xo_hi[:, 2 * b:2 * b + 2, :].bitcast(F32), ALU.subtract).then_inc(x_olo, 1)
            for c in range(CH):
                for k in range(2):
                    lo(U_XO + 2 * c + k + LEAD)
                if c:
                    turn_low(T_X2 + c - 1, a_lo, a_hi, 4 * (c - 1), V_FFN)
                dve.wait_ge(used, U_XO + 2 * (c + 1))
                add_to_residual(N_XO + c, c)
            turn_low(T_X2 + CH - 1, a_lo, a_hi, 4 * (CH - 1), V_FFN)
            add_parts(SS_2, 3)
            reciprocal(rs_2, sd_n, R_2)

            def ff_group(g, r, last):
                for c in range(CH):
                    for k in range(UPC):
                        lo(U_FF + UPC * c + k + LEAD, r)
                        if k == 3 and c:
                            turn_low(g * CH + (T_FF + c - 1), c_lo, c_hi, 4 * (c - 1))
                    p = pair_of(N_FF + c)
                    dve.wait_ge(relu_ready, g * CH + (c + 1))
                    dve.tensor_tensor(rows[:, p, :, :], rows[:, p, :, :], rows[:, p, :, :], ALU.mult).then_inc(chunk_out, 1)
                for c in range(CH):
                    for k in range(UPC):
                        if not last or UPC * (CH + c) + k + LEAD < FF_UNITS:
                            lo(U_FF + UPC * (CH + c) + k + LEAD, r)
                        if k == 3 and c == 0:
                            turn_low(g * CH + (T_FF + CH - 1), c_lo, c_hi, 4 * (CH - 1))
                    dve.wait_ge(used, r + (U_FF + UPC * (CH + c + 1)))
                    add_to_residual(N_FF + CH + c, c)

            with dve.Fori(0, GROUPS - 1) as g:
                ff_group(g, g * FF_UNITS, False)
            ff_group(GROUPS - 1, (GROUPS - 1) * FF_UNITS, True)
            add_parts(SS_3, 4)
            reciprocal(rs_3, sd_n, R_3)
            dve.wait_ge(rs_ready, R_3)
            dve.wait_ge(fin_landed, 16)
            for c in range(CH):
                for t in range(TT):
                    cols = slice(NC * c, NC * (c + 1))
                    last = dve.scalar_tensor_tensor(out=fin[:, t, cols], in0=xres[:, t, cols], scalar=rs_3[:, t:t + 1], in1=fin_g[:, cols],
                                                    op0=ALU.mult, op1=ALU.mult)
                last.then_inc(fin_ready, 1)

        @block.tensor
        def _(pe):
            def unit(u, r, x_hi, x_lo, k0, bank, first, last, kts=2, width=NC):
                s = u % RING
                pe.wait_ge(lo_ready, u + 1 + r)
                for k in range(kts):
                    for t in range(TT):
                        sum_ = ps[:, bank + t, 0:width]
                        tok = slice(P * t, P * (t + 1))
                        w_hi, w_lo = (w[:, s, width * k:width * (k + 1)] for w in (whi, wlo))
                        pe.matmul(sum_, x_hi[:, k0 + k, tok], w_hi, start=(first and k == 0), stop=False)
                        pe.matmul(sum_, x_hi[:, k0 + k, tok], w_lo, start=False, stop=False)
                        mm = pe.matmul(sum_, x_lo[:, k0 + k, tok], w_hi, start=False, stop=(last and k == kts - 1))
                mm.then_inc(used, 1)

            def turn(n, src, c0, after=None):
                for b in range(2):
                    if after is not None:
                        pe.wait_ge(after[0], after[1] + b)
                    for k in (2 * b, 2 * b + 1):
                        for t in range(TT):
                            tr = pe.transpose(ps[:, 6 + b, SEQ * (k % 2) + P * t:SEQ * (k % 2) + P * (t + 1)],
                                              src[:, t, c0 + P * k:c0 + P * (k + 1)], ident[:])
                    tr.then_inc(turned, 1)

            def split_out(n):
                return turn_lo, 2 * splits_before(n) + 1

            def copied_out(n):
                return turn_hi, n * 2 + 1

            pe.wait_ge(consts, 2)
            pe.wait_ge(vec_landed, 16 * 8)
            pe.transpose(ps[:, 5, 0:V_N], vec_rows[0:V_N, :], ident[0:V_N, 0:V_N]).then_inc(vec_turned, 1)
            pe.wait_ge(x_landed, 16 * TT)
            turn(T_X, x_in, 0)
            turn(T_X + 1, x_in, NC, split_out(T_X))
            for k in range(UPC):
                if k in (2, 4):
                    turn(T_X + 1 + k // 2, x_in, NC * (1 + k // 2), split_out(T_X + k // 2))
                pe.wait_ge(turn_lo, k + 1)
                unit(U_CONV + k, 0, a_hi, a_lo, 2 * k, 2, k == 0, k == UPC - 1)
            pe.wait_ge(cw_landed, 32)
            for k in range(KT):
                tr = pe.transpose(ps[:, 4, (CONV_K + 1) * k:(CONV_K + 1) * (k + 1)], cw_rows[:, P * k:P * (k + 1)],
                                  ident[0:CONV_K + 1, 0:CONV_K + 1])
            tr.then_inc(cw_turned, 1)
            for k in range(UPC):
                unit(U_CONV + UPC + k, 0, a_hi, a_lo, 2 * k, 0, k == 0, k == UPC - 1)

            with pe.Fori(1, CH) as i:
                r = i * (2 * UPC)
                pe.wait_ge(sg_ready, i)
                for k in range(UPC):
                    unit(U_CONV + k, r, a_hi, a_lo, 2 * k, 2, k == 0, k == UPC - 1)
                    if k == 2:
                        pe.wait_ge(chunk_out, i)
                        pe.wait_ge(turn_lo, 2 * CH)
                        turn(i + (T_CONV - 1), rows[:, 0, :, :], 0, (turn_hi, i * 2 + (2 * (T_CONV - 2) + 1)))
                for k in range(UPC):
                    unit(U_CONV + UPC + k, r, a_hi, a_lo, 2 * k, 0, k == 0, k == UPC - 1)

            pe.wait_ge(sg_ready, CH)
            for k in range(UPC):
                unit(U_LORA + k, 0, a_hi, a_lo, 2 * k, 2, k == 0, k == UPC - 1)
                if k == 2:
                    pe.wait_ge(chunk_out, N_CQ)
                    turn(T_CONV + CH - 1, rows[:, 0, :, :], 0, copied_out(T_CONV + CH - 2))
            for k in range(UPC):
                unit(U_LORA + UPC + k, 0, a_hi, a_lo, 2 * k, 0, k == 0, k == UPC - 1)
                if k == 2:
                    pe.wait_ge(chunk_out, N_CQ + 1)
                    turn(T_CQ, rows[:, 0, :, :], 0, copied_out(T_CQ - 1))
            pe.wait_ge(conv_step, 1)
            unit(U_KPE, 0, a_hi, a_lo, 0, 4, True, True, KT, ROPE)
            pe.wait_ge(chunk_out, N_CKV + 1)
            turn(T_CKV, rows[:, 1, :, :], 0, split_out(T_CQ))
            pe.wait_ge(kpe_rotated, 2)
            for t in range(TT):
                tr = pe.transpose(ps[0:ROPE, 5, P * t:P * (t + 1)], kpe_rot[:, t, :], ident[:])
            tr.then_inc(kpe_turned, 1)
            pe.wait_ge(turn_lo, 2 * splits_before(T_CKV) + 2)
            pe.wait_ge(kpeT_ready, 1)

            with pe.Fori(0, PAIRS) as j:
                r = j * ATT_UNITS

                def gate_unit(k):
                    unit(U_ATT + 4 + k, r, a_hi, a_lo, 2 * k, 0, k == 0, k == UPC - 1)

                for n in range(2):
                    unit(U_ATT + n, r, cq_hi, cq_lo, 2 * n, 2, n == 0, n == 1, 2, QW)
                for n in range(2):
                    unit(U_ATT + 2 + n, r, ckv_hi, ckv_lo, 2 * n, 4, n == 0, n == 1)
                pe.wait_ge(chunk_out, j + N_GATE)
                gate_unit(0)
                gate_unit(1)
                pe.wait_ge(q_rotated, j * 4 + 4)
                for h in range(2):
                    a = h * (NOPE + ROPE)
                    for t in range(TT):
                        tr = pe.transpose(ps[:, 6, SEQ * h + P * t:SEQ * h + P * (t + 1)], q_row[:, t, a:a + NOPE], ident[:])
                tr.then_inc(qk_turned, 1)
                pe.wait_ge(kv_ready, j + 1)
                for h in range(2):
                    a = h * (NOPE + VD)
                    for t in range(TT):
                        tr = pe.transpose(ps[:, 7, SEQ * h + P * t:SEQ * h + P * (t + 1)], kv_row[:, t, a:a + NOPE], ident[:])
                tr.then_inc(qk_turned, 1)
                for h in range(2):
                    a = h * (NOPE + ROPE) + NOPE
                    for t in range(TT):
                        tr = pe.transpose(ps[0:ROPE, 2, SEQ * h + P * t:SEQ * h + P * (t + 1)], q_row[:, t, a:a + ROPE], ident[:])
                tr.then_inc(qk_turned, 1)
                gate_unit(2)
                pe.wait_ge(qT_ready, j * 2 + 2)
                pe.wait_ge(kT_ready, j + 1)
                for h in range(2):
                    for t in range(TT):
                        keys = P * (t + 1)
                        sc = ps[:, 3 + h, P * t:P * t + keys]
                        tok = slice(P * t, P * (t + 1))
                        pe.matmul(sc, qT[:, h, tok], kT[:, h, 0:keys], start=True, stop=False)
                        mm = pe.matmul(sc, qrT[:, h, tok], kpeT[:, 0:keys], start=False, stop=True)
                    mm.then_inc(scored, 1)
                gate_unit(3)
                gate_unit(4)
                gate_unit(5)
                for h in range(2):
                    pe.wait_ge(probs_ready, j * 4 + 2 * (h + 1))
                    for n in range(3):
                        tr = pe.transpose(ps[:, 5 + h, P * n:P * (n + 1)], probs[:, h, P * n:P * (n + 1)], ident[:])
                    tr.then_inc(p_turned, 1)
                gate_unit(6)
                pe.wait_ge(pT_ready, j * 2 + 2)
                for h in range(2):
                    a = h * (NOPE + VD) + NOPE
                    pe.matmul(ps[:, 7, SEQ * h:SEQ * (h + 1)], kv_row[:, 0, a:a + VD], pT[:, h, 0:SEQ], start=True, stop=False)
                    mm = pe.matmul(ps[:, 7, SEQ * h + P:SEQ * (h + 1)], kv_row[:, 1, a:a + VD], pT[:, h, SEQ:SW], start=False, stop=True)
                mm.then_inc(o_ready, 1)
                gate_unit(7)

            pe.wait_ge(o_lo, PAIRS)
            for c in range(CH):
                n = N_MLA + c
                if c:
                    pe.wait_ge(chunk_out, n - 1)
                for k in range(UPC):
                    unit(U_MLA + UPC * c + k, 0, c_hi, c_lo, 2 * k, 2 * pair_of(n), k == 0, k == UPC - 1)
                    if c == CH - 1 and k == 5:
                        pe.wait_ge(mean_ready, 1)
                        pe.wait_ge(ln_added, 5)
                        pe.matmul(ps[:, 4, 0:SEQ], mean_w[:], ln_sum[:, 0, :], start=True, stop=True).then_inc(ln_mean, 1)
                    if k == 2:
                        pe.wait_ge(mem_landed[c % 2], 16 * (c // 2 + 1))
                        turn(T_MEM + c, rows[:, c % 2, :, :], 0, split_out(T_MEM + c - 1) if c else None)

            for n in (N_XK, N_XV):
                u = U_XKV + UPC * (n - N_XK)
                pe.wait_ge(chunk_out, n - 1)
                for k in range(UPC):
                    if n == N_XK:
                        pe.wait_ge(turn_lo, 2 * splits_before(T_MEM) + k + 1)
                    unit(u + k, 0, m_hi, m_lo, 2 * k, 2 * pair_of(n), k == 0, k == UPC - 1)
                    if n == N_XK and k == 6:
                        pe.wait_ge(ln_added, 10)
                        pe.matmul(ps[:, 5, 0:SEQ], mean_w[:], ln_sum[:, 0, :], start=True, stop=True).then_inc(ln_var, 1)

            for c in range(CH):
                n = N_COUT + c
                pe.wait_ge(chunk_out, n - 1)
                for k in range(UPC):
                    if c == 0:
                        pe.wait_ge(st_lo, k // 2 + 1)
                    unit(U_COUT + UPC * c + k, 0, a_hi, a_lo, 2 * k, 2 * pair_of(n), k == 0, k == UPC - 1)
                    if k == 3 and c == 0:
                        turn(T_XK, rows[:, pair_of(N_XK), :, :], 0, split_out(T_XK - 1))
                    if k == 3 and c:
                        pe.wait_ge(chunk_out, n)
                        turn(T_MRG + c - 1, rows[:, pair_of(n - 1), :, :], 0, copied_out(T_XK) if c == 1 else split_out(T_MRG + c - 2))

            for c in range(CH):
                n = N_WOUT + c
                pe.wait_ge(chunk_out, n - 1)
                for k in range(UPC):
                    if c == 0:
                        pe.wait_ge(turn_lo, 2 * splits_before(T_MRG) + k + 1)
                    unit(U_WOUT + UPC * c + k, 0, c_hi, c_lo, 2 * k, 2 * pair_of(n), k == 0, k == UPC - 1)
                    if k == 3:
                        pe.wait_ge(chunk_out, n)
                        if c == 0:
                            turn(T_MRG + CH - 1, rows[:, pair_of(n - 1), :, :], 0, split_out(T_MRG + CH - 2))
                        else:
                            turn(T_X1 + c - 1, xres, NC * (c - 1), split_out(T_X1 + c - 2))

            pe.wait_ge(chunk_out, N_XQ - 1)
            for k in range(UPC):
                pe.wait_ge(turn_lo, 2 * splits_before(T_X1) + k + 1)
                unit(U_XQ + k, 0, a_hi, a_lo, 2 * k, 2 * pair_of(N_XQ), k == 0, k == UPC - 1)
                if k == 3:
                    pe.wait_ge(chunk_out, N_XQ)
                    turn(T_X1 + CH - 1, xres, NC * (CH - 1), split_out(T_X1 + CH - 2))
            pe.wait_ge(chunk_out, N_XQ + 1)
            turn(T_XQ, rows[:, pair_of(N_XQ), :, :], 0, split_out(T_XQ - 1))
            pe.wait_ge(turn_hi, 2 * T_XQ + 2)
            for h in range(XH):
                for t in range(TT):
                    mm = pe.matmul(ps[:, h, SEQ * t:SEQ * (t + 1)], xqT[:, h, P * t:P * (t + 1)], xkT[:, h, :], start=True, stop=True)
                mm.then_inc(x_scored, 1)
            for h in range(XH):
                pe.wait_ge(x_probs, TT * (h + 1))
                for k in range(TT):
                    for t in range(TT):
                        tr = pe.transpose(ps[:, 4 + h, SEQ * k + P * t:SEQ * k + P * (t + 1)], xp[:, h, t, P * k:P * (k + 1)], ident[:])
                tr.then_inc(x_pturned, 1)
            for h in range(XH):
                pe.wait_ge(x_pT, h + 1)
                for k in range(TT):
                    mm = pe.matmul(ps[:, h // 2, SEQ * (h % 2):SEQ * (h % 2 + 1)], xv[:, k, P * h:P * (h + 1)], xpT[:, h, k, :],
                                   start=(k == 0), stop=(k == TT - 1))
                if h % 2:
                    mm.then_inc(x_o, 1)
            pe.wait_ge(x_olo, 2)
            for c in range(CH):
                n = N_XO + c
                pe.wait_ge(chunk_out, n - 1)
                for k in range(2):
                    unit(U_XO + 2 * c + k, 0, xo_hi, xo_lo, 2 * k, 2 * pair_of(n), k == 0, k == 1)
                if c:
                    pe.wait_ge(chunk_out, n)
                    turn(T_X2 + c - 1, xres, NC * (c - 1), split_out(T_X2 + c - 2) if c > 1 else None)
            pe.wait_ge(chunk_out, N_XO + CH)
            turn(T_X2 + CH - 1, xres, NC * (CH - 1), split_out(T_X2 + CH - 2))

            with pe.Fori(0, GROUPS) as g:
                r = g * FF_UNITS
                for c in range(2 * CH):
                    n = N_FF + c
                    p = pair_of(n)
                    pe.wait_ge(chunk_out, g * (2 * CH) + (n - 1))
                    for k in range(UPC):
                        if c == 0:
                            pe.wait_ge(turn_lo, 2 * splits_before(T_X2) + k + 1)
                        if c == CH:
                            pe.wait_ge(turn_lo, g * (2 * CH) + (2 * splits_before(T_FF) + k + 1))
                        x_hi, x_lo = (a_hi, a_lo) if c < CH else (c_hi, c_lo)
                        unit(U_FF + UPC * c + k, r, x_hi, x_lo, 2 * k, 2 * p, k == 0, k == UPC - 1)
                        if k == 3 and 1 <= c <= CH:
                            pe.wait_ge(chunk_out, g * (2 * CH) + n)
                            turn(None, rows[:, pair_of(n - 1), :, :], 0,
                                 (turn_lo, g * (2 * CH) + (2 * splits_before(T_FF + c - 2) + 1)))


_INS = ['x', 'mem', 'positions', 'norm_mix_g', 'w_in', 'b_gate', 'conv_w', 'conv_b', 'conv_ln_g', 'conv_ln_b',
        'w_conv_out', 'q_norm_g', 'w_uq', 'kv_norm_g', 'w_ukv', 'w_mla_out', 'w_out', 'norm_mem_g', 'mem_norm_g',
        'w_xq', 'w_xkv', 'w_xo', 'norm_ffn_g', 'w_ff1', 'w_ff2', 'final_norm_g']
_OUTS = [((1, SEQ, D), 'float32')]


def kernel(**inputs):
    import numpy as _np
    import concourse.bacc as _bacc
    from concourse import mybir as _mybir
    from concourse.bass_utils import run_bass_kernel_spmd as _run

    nc = _bacc.Bacc("TRN2", target_bir_lowering=False, num_devices=1)
    arrays, args = {}, []
    for name in _INS:
        a = _np.ascontiguousarray(inputs[name])
        arrays[f"in_{name}_dram"] = a
        args.append(nc.dram_tensor(f"in_{name}_dram", a.shape, _mybir.dt.from_np(a.dtype), kind="ExternalInput").ap())
    for i, (shape, dtype) in enumerate(_OUTS):
        dt = _mybir.dt.from_np(_np.dtype(dtype))
        args.append(nc.dram_tensor(f"out_{i}_dram", shape, dt, kind="ExternalOutput").ap())
    build(nc, *args)
    r = _run(nc, [arrays], core_ids=[0])
    got = tuple(r.results[0][f"out_{i}_dram"] for i in range(len(_OUTS)))
    return got[0]
```

```python
from contextlib import ExitStack

import numpy as np

import concourse.bass as bass
from concourse import mybir

ALU = mybir.AluOpType
ACT = mybir.ActivationFunctionType
AX_X = mybir.AxisListType.X
F32 = mybir.dt.float32
F32R = mybir.dt.float32r
I32 = mybir.dt.int32
ds = bass.ds

P = 128
D = 2048
SEQ = 256
TT = SEQ // P
KT = D // P
NC = 512
CH = D // NC
CPB = NC // P
CONV_K = 31
PAD = CONV_K - 1
HC = SEQ + PAD
LORA = 512
LT = LORA // P
NOPE, ROPE, VD = 128, 64, 128
HALF = ROPE // 2
HEADS = 16
PAIRS = HEADS // 2
QW = 2 * (NOPE + ROPE)
KVW = 2 * (NOPE + VD)
XH = 4
DFF = 4 * D
SW = P + SEQ
SCORES = [(0, 0, P), (0, P, SW), (1, 0, P), (1, P, SW)]
GROUPS = DFF // D
EPS = 1e-6
NEG = -3.0e38
SM = float(NOPE + ROPE) ** -0.5
XSM = 128.0 ** -0.5
COL_A, COL_G, COL_CQ, COL_CKV = 0, D, 2 * D, 2 * D + LORA
COL_KPE = COL_CKV + LORA
COL_GATE = COL_KPE + ROPE

UE = 2 * NC
RING = 4
LEAD = 3
UPC = KT // 2
U_CONV = 0
U_CQ = U_CONV + 2 * CH * UPC
U_KPE = U_CQ + UPC
U_CKV = U_KPE + 1
U_ATT = U_CKV + UPC
ATT_UNITS = 4 + UPC
U_MLA = U_ATT + PAIRS * ATT_UNITS
U_XKV = U_MLA + CH * UPC
U_COUT = U_XKV + 2 * UPC
U_WOUT = U_COUT + CH * UPC
U_XQ = U_WOUT + CH * UPC
U_XO = U_XQ + UPC
U_FF = U_XO + CH * 2
FF_UNITS = 2 * CH * UPC
U_END = U_FF + GROUPS * FF_UNITS

T_X = 0
T_CONV = T_X + CH
T_CQ = T_CONV + CH
T_CKV = T_CQ + 1
T_MEM = T_CKV + 1
T_XK = T_MEM + CH
T_MRG = T_XK + 1
T_X1 = T_MRG + CH
T_XQ = T_X1 + CH
T_X2 = T_XQ + 1
T_FF = T_X2 + CH


def splits_before(turn):
    return turn - CH * (turn > T_CONV) - (turn > T_XK) - (turn > T_XQ)


N_CONV = 0
N_CQ = N_CONV + CH
N_CKV = N_CQ + 1
N_GATE = N_CKV + 1
N_MLA = N_GATE + PAIRS
N_XK = N_MLA + CH
N_XV = N_XK + 1
N_COUT = N_XV + 1
N_WOUT = N_COUT + CH
N_XQ = N_WOUT + CH
N_XO = N_XQ + 1
N_FF = N_XO + CH

R_X, R_Q, R_KV, R_MEM, R_1, R_2, R_3 = range(1, 8)
SS_X = TT
SS_Q = SS_X + TT
SS_KV = SS_Q + TT
SS_MEM = SS_KV + TT * CH
SS_1 = SS_MEM + TT * CH
SS_2 = SS_1 + TT * CH
SS_3 = SS_2 + TT * CH
CONV_STEPS = CONV_K + 2
CONV_A, CONV_B = 4, 2
CONV_D = KT - CONV_A - CONV_B - PAIRS


X_BEFORE, X_AFTER = (1, 2, 4), (2, 3, 5)


def pair_of(n):
    return (n + 1) % 2


V_MIX, V_LG, V_LB, V_NMEM, V_MEMN, V_FFN = (KT * n for n in range(6))
V_QG = 6 * KT
V_KG = V_QG + LT
V_N = V_KG + LT

PI_NUM, PI_DEN = 31415926535897932384626433832795028841971693993751058209749445923, 10 ** 64
MAGIC = 1.5 * 2.0 ** 23
TWO_PI = 6.283185


def turn_pieces(n):
    num, den, out = PI_DEN, 2 * PI_NUM, []
    for k in range(n):
        bits = 14 + 12 * k
        piece = (num << bits) // den
        out.append(piece / 2.0 ** bits)
        num, den = (num << bits) - piece * den, den << bits
    return out


def inv_freqs():
    exponent = np.arange(0, ROPE, 2, dtype=np.float32) / np.float32(ROPE)
    return [float(v) for v in np.float32(1.0) / np.power(np.float32(10000.0), exponent)]


def nbytes(shape):
    n = 4
    for s in shape[1:]:
        n *= s
    return n


def build(nc, x, mem, positions, norm_mix_g, w_in, b_gate, conv_w, conv_b, conv_ln_g, conv_ln_b,
          w_conv_out, q_norm_g, w_uq, kv_norm_g, w_ukv, w_mla_out, w_out, norm_mem_g, mem_norm_g,
          w_xq, w_xkv, w_xo, norm_ffn_g, w_ff1, w_ff2, final_norm_g, out):
    def k_rows(w):
        return w.rearrange("o (k p) n -> p (o k) n", p=P)

    w_in, w_uq, w_ukv, w_mla_out, w_conv_out, w_out = (k_rows(w) for w in (w_in, w_uq, w_ukv, w_mla_out, w_conv_out, w_out))
    w_xq, w_xkv, w_xo, w_ff1, w_ff2 = (k_rows(w) for w in (w_xq, w_xkv, w_xo, w_ff1, w_ff2))
    x_v, mem_v, out_v = (v.rearrange("o (t p) n -> p (o t) n", p=P) for v in (x, mem, out))

    with ExitStack() as ctx:
        cursor = [(nc.sbuf_base + 31) // 32 * 32]

        def at(offset, name, shape, dt=F32):
            return nc.alloc_sbuf_tensor_at(name, shape, dt, offset=offset)

        def take(name, shape, dt=F32):
            offset = cursor[0]
            cursor[0] += (nbytes(shape) + 31) // 32 * 32
            return at(offset, name, shape, dt)

        KS = nbytes([P, KT, SEQ])
        raw = take("raw", [P, RING, UE])
        whi = take("whi", [P, RING, UE], F32R)
        wlo = take("wlo", [P, RING, UE], F32R)
        o = cursor[0]
        a_hi = take("a_hi", [P, KT, SEQ], F32R)
        a_lo = take("a_lo", [P, KT, SEQ], F32R)
        ln_sq = at(o, "ln_sq", [P, KT, SEQ])
        ln_sum = at(o + KS, "ln_sum", [P, KT // 2, SEQ])
        sq_mem = at(o + KS + KS // 2, "sq_mem", [P, TT, NC])
        o = cursor[0]
        c_hi = take("c_hi", [P, KT, SEQ], F32R)
        c_lo = take("c_lo", [P, KT, SEQ], F32R)
        cw_rows = at(o, "cw_rows", [CONV_K + 1, D])
        sq_x = at(o + nbytes([P, D]), "sq_x", [P, TT, D])
        o = cursor[0]
        gates = take("gates", [P, TT, 2 * D])
        x_in = at(o, "x_in", [P, TT, D])
        vec_rows = at(o + KS, "vec_rows", [P, P])
        rope_tmp = at(o + KS + 512, "rope_tmp", [P, 6, TT * HALF])
        xo_hi = at(o, "xo_hi", [P, XH, SEQ], F32R)
        xo_lo = at(o + 4096, "xo_lo", [P, XH, SEQ], F32R)
        fin_g = at(o + 8192, "fin_g", [P, D])
        fin = at(o + KS, "fin", [P, TT, D])
        o = cursor[0]
        m_hi = take("m_hi", [P, KT, SEQ], F32R)
        m_lo = take("m_lo", [P, KT, SEQ], F32R)
        cq_hi = at(o, "cq_hi", [P, LT, SEQ], F32R)
        cq_lo = at(o + 4096, "cq_lo", [P, LT, SEQ], F32R)
        ckv_hi = at(o + 8192, "ckv_hi", [P, LT, SEQ], F32R)
        ckv_lo = at(o + 12288, "ckv_lo", [P, LT, SEQ], F32R)
        kv_row = at(o + 16384, "kv_row", [P, TT, KVW])
        sq_lat = at(o + 16384, "sq_lat", [P, TT, LORA])
        qT = at(o + 20480, "qT", [P, 2, SEQ])
        kT = at(o + 22528, "kT", [P, 2, SEQ])
        qrT = at(o + 24576, "qrT", [ROPE, 2, SEQ])
        kpeT = at(o + 26624, "kpeT", [ROPE, SEQ])
        mask = at(o + 27648, "mask", [P, SW])
        kpe_sum = at(o + 20480, "kpe_sum", [ROPE, SEQ])
        kpe_row = at(o + 29184, "kpe_row", [P, TT, ROPE])
        kpe_rot = at(o + 29696, "kpe_rot", [P, TT, ROPE])
        rot = at(o + 30208, "rot", [P, 4, 2, TT, HALF])
        xkT = at(o, "xkT", [P, XH, SEQ])
        xv = at(o + 4096, "xv", [P, TT, XH * P])
        xqT = at(o + 8192, "xqT", [P, XH, SEQ])
        xp = at(o + 12288, "xp", [P, XH, TT, SEQ])
        sq_res = at(o + 12288, "sq_res", [P, TT, NC])
        xpT = at(o + 20480, "xpT", [P, XH, TT, SEQ])
        o = cursor[0]
        hconv = take("hconv", [P, KT, HC])
        xres = at(o, "xres", [P, TT, D])
        o = cursor[0]
        acc = take("acc", [P, 2, SEQ])
        mean_w = at(o + 4 * SEQ, "mean_w", [P, P])
        o = cursor[0]
        rows = take("rows", [P, 2, TT, NC])
        q_row = at(o, "q_row", [P, TT, QW])
        pT = at(o, "pT", [P, 2, SW])
        probs = at(o + 3072, "probs", [P, 2, SW])
        gbias = at(o + 6144, "gbias", [P, NC])

        cw = take("cw", [P, KT, CONV_K + 1])
        cwk = take("cwk", [P, CONV_K + 1])
        ident = take("ident", [P, P])
        vec = take("vec", [P, V_N])
        rope_cs = take("rope_cs", [P, 2, TT, HALF])
        stat = take("stat", [P, 80])
        pos_i = take("pos_i", [P, TT], I32)
        assert cursor[0] <= nc.sbuf_usable_end, (cursor[0], nc.sbuf_usable_end)

        def st(n, w=TT):
            return stat[:, n:n + w]

        eps = st(0, 1)
        ss_x, sd_x, rs_x = st(2), st(4), st(6)
        ss_q, sd_q, rs_q = st(8), st(10), st(12)
        ss_kv, sd_kv, rs_kv = st(14), st(16), st(18)
        ss_part = stat[:, 20:28].rearrange("p (t c) -> p t c", t=TT)
        ss_sum, sd_n = st(28), st(30)
        rs_mem, rs_1, rs_2, rs_3 = st(32), st(34), st(36), st(38)
        top, ntop, den, rden = st(40, 4), st(44, 4), st(48, 4), st(52, 4)
        xtop, xntop, xden, xrden = st(56, 8), st(40, 8), st(64, 8), st(72, 8)

        ps = ctx.enter_context(nc.psum_tensor("ps", [P, 8, NC], F32))

        def sem(name):
            return ctx.enter_context(nc.semaphore(name))

        landed = [sem(f"landed{n}") for n in range(RING)]
        hi_ready = sem("hi_ready")
        lo_ready = sem("lo_ready")
        used = sem("used")
        chunk_out = sem("chunk_out")
        turned = sem("turned")
        turn_hi = sem("turn_hi")
        turn_lo = sem("turn_lo")
        x_landed = [sem(f"x_landed{n}") for n in range(CH)]
        mix_landed, vec_landed, cw_landed, pos_landed = (sem(n) for n in ("mix_landed", "vec_landed", "cw_landed", "pos_landed"))
        consts, mask_ready, mean_ready = sem("consts"), sem("mask_ready"), sem("mean_ready")
        vec_turned, vec_ready, cw_turned = (sem(n) for n in ("vec_turned", "vec_ready", "cw_turned"))
        angle_step, angle_ready, rope_ready = (sem(n) for n in ("angle_step", "angle_ready", "rope_ready"))
        ss_ready, sum_ready, sd_ready, rs_ready = (sem(n) for n in ("ss_ready", "sum_ready", "sd_ready", "rs_ready"))
        sg_ready = sem("sg_ready")
        conv_step = sem("conv_step")
        ln_added, ln_mean, ln_centred, ln_squared, ln_var = (sem(n) for n in ("ln_added", "ln_mean", "ln_centred", "ln_squared", "ln_var"))
        ln_root, ln_scaled, silu_done, st_hi, st_lo = (sem(n) for n in ("ln_root", "ln_scaled", "silu_done", "st_hi", "st_lo"))
        kpe_out, kpe_ready, kpe_prod, kpe_rotated, kpe_turned, kpeT_ready = (sem(n) for n in ("kpe_out", "kpe_ready", "kpe_prod", "kpe_rotated", "kpe_turned", "kpeT_ready"))
        q_ready, kv_ready, q_prod, q_rotated = (sem(n) for n in ("q_ready", "kv_ready", "q_prod", "q_rotated"))
        qk_turned, qT_ready, kT_ready = (sem(n) for n in ("qk_turned", "qT_ready", "kT_ready"))
        scored, masked, ntop_ready = (sem(n) for n in ("scored", "masked", "ntop_ready"))
        exp_ready, rden_ready, probs_ready = (sem(n) for n in ("exp_ready", "rden_ready", "probs_ready"))
        p_turned, pT_ready = sem("p_turned"), sem("pT_ready")
        o_ready, o_hi, o_lo = (sem(n) for n in ("o_ready", "o_hi", "o_lo"))
        bias_landed, gate_ready = sem("bias_landed"), sem("gate_ready")
        mem_landed = [sem("mem_landed0"), sem("mem_landed1")]
        gated, res_landed = sem("gated"), sem("res_landed")
        xq_row = sem("xq_row")
        x_scored, x_top, x_ntop, x_exp, x_rden, x_probs = (sem(n) for n in ("x_scored", "x_top", "x_ntop", "x_exp", "x_rden", "x_probs"))
        x_pturned, x_pT, x_o, x_ohi, x_olo = (sem(n) for n in ("x_pturned", "x_pT", "x_o", "x_ohi", "x_olo"))
        relu_ready, fin_landed, last_rows, fin_gained = (sem(n) for n in ("relu_ready", "fin_landed", "last_rows", "fin_gained"))
        fin_act, fin_dve, stored = sem("fin_act"), sem("fin_dve"), sem("stored")

        block = ctx.enter_context(nc.Block())

        def wait(eng, s, value):
            if not isinstance(value, int) or value > 0:
                eng.wait_ge(s, value)

        @block.sync
        def _(sp):
            def load(u, r, src, kts=2, width=NC):
                wait(sp, lo_ready, u - RING + 1 + r)
                sp.dma_start(raw[:, u % RING, 0:kts * width].rearrange("p (k n) -> p k n", k=kts),
                             src).then_inc(landed[u % RING], 16)

            def load_x(c):
                sp.dma_start(x_in[:, :, NC * c:NC * (c + 1)], x_v[:, :, NC * c:NC * (c + 1)]).then_inc(x_landed[c], 16)

            def load_chunk(u, r, w, col):
                for k in range(UPC):
                    load(u + k, r, w[:, 2 * k:2 * k + 2, ds(col, NC)])

            for k in range(UPC):
                if k in (0, 1, 3):
                    load_x((0, 1, 3).index(k))
                load(U_CONV + k, 0, w_in[:, 2 * k:2 * k + 2, COL_G:COL_G + NC])
                if k == 3:
                    load_x(3)
            load_chunk(U_CONV + UPC, 0, w_in, COL_A)
            with sp.Fori(0, CH - 1) as i:
                load_chunk(U_CONV + 2 * UPC, i * (2 * UPC), w_in, i * NC + (COL_G + NC))
                load_chunk(U_CONV + 3 * UPC, i * (2 * UPC), w_in, i * NC + (COL_A + NC))
            load_chunk(U_CQ, 0, w_in, COL_CQ)
            load(U_KPE, 0, w_in[:, :, COL_KPE:COL_KPE + ROPE], KT, ROPE)
            load_chunk(U_CKV, 0, w_in, COL_CKV)

            with sp.Fori(0, PAIRS) as j:
                r = j * ATT_UNITS
                for n in range(2):
                    load(U_ATT + n, r, w_uq[:, 2 * n:2 * n + 2, ds(j * QW, QW)], 2, QW)
                for n in range(2):
                    load(U_ATT + 2 + n, r, w_ukv[:, 2 * n:2 * n + 2, ds(j * KVW, KVW)])
                load_chunk(U_ATT + 4, r, w_in, j * NC + COL_GATE)
                sp.wait_ge(turned, 2 * (T_CKV + 1))
                sp.wait_ge(chunk_out, j + N_GATE)
                sp.dma_start(gbias[:], b_gate[:, ds(j * NC, NC)].to_broadcast([P, NC])).then_inc(bias_landed, 16)

            for c in range(CH):
                load_chunk(U_MLA + UPC * c, 0, w_mla_out, NC * c)
            for c in range(2):
                load_chunk(U_XKV + UPC * c, 0, w_xkv, NC * c)
            for c in range(CH):
                load_chunk(U_COUT + UPC * c, 0, w_conv_out, NC * c)
            sp.wait_ge(st_lo, KT // 4)
            sp.dma_start(xres[:], x_v).then_inc(res_landed, 16)
            for c in range(CH):
                load_chunk(U_WOUT + UPC * c, 0, w_out, NC * c)
            load_chunk(U_XQ, 0, w_xq, 0)
            for c in range(CH):
                for n in range(2):
                    load(U_XO + 2 * c + n, 0, w_xo[:, 2 * n:2 * n + 2, NC * c:NC * (c + 1)])
            with sp.Fori(0, GROUPS) as g:
                r = g * FF_UNITS
                for c in range(CH):
                    load_chunk(U_FF + UPC * c, r, w_ff1, g * D + NC * c)
                for c in range(CH):
                    for k in range(UPC):
                        load(U_FF + UPC * (CH + c) + k, r, w_ff2[:, ds(g * KT + 2 * k, 2), NC * c:NC * (c + 1)])
            for c, ready, n in ((2, fin_dve, 1), (0, fin_act, 1), (3, fin_dve, 2), (1, fin_act, 2)):
                sp.wait_ge(ready, n)
                sp.dma_start(out_v[:, :, NC * c:NC * (c + 1)], fin[:, :, NC * c:NC * (c + 1)]).then_inc(stored, 16)
            sp.wait_ge(stored, 16 * CH)

        @block.gpsimd
        def _(pool):
            def vector_rows(v):
                return v.rearrange("o (k p) -> (o k) p", p=P)

            pool.memset(ident[:], 0.0).then_inc(consts, 1)
            pool.wait_ge(consts, 1)
            pool.affine_select(out=ident[:], in_=ident[:], compare_op=ALU.not_equal, fill=1.0, base=0,
                               pattern=[[-1, P]], channel_multiplier=1).then_inc(consts, 1)
            pool.memset(eps, EPS).then_inc(consts, 1)
            for n, v in enumerate((conv_ln_g, conv_ln_b, norm_mem_g, mem_norm_g, norm_ffn_g)):
                pool.dma_start(vec_rows[KT * (n + 1):KT * (n + 2), :], vector_rows(v)).then_inc(vec_landed, 16)
            pool.dma_start(vec_rows[V_QG:V_QG + LT, :], vector_rows(q_norm_g)).then_inc(vec_landed, 16)
            pool.dma_start(vec_rows[V_KG:V_KG + LT, :], vector_rows(kv_norm_g)).then_inc(vec_landed, 16)
            pool.dma_start(cw_rows[0:CONV_K, :], conv_w.rearrange("o k n -> (o k) n")).then_inc(cw_landed, 16)
            pool.dma_start(cw_rows[CONV_K:CONV_K + 1, :], conv_b).then_inc(cw_landed, 16)
            pool.dma_start(pos_i[:], positions.rearrange("o (t p) -> p (o t)", p=P), allow_slow_non_contiguous=True).then_inc(pos_landed, 16)
            pool.memset(hconv[:, :, 0:PAD], 0.0).then_inc(consts, 1)
            pool.memset(mask[:], 0.0).then_inc(mask_ready, 1)
            pool.wait_ge(mask_ready, 1)
            pool.memset(mask[0:64, 64:128], NEG).then_inc(mask_ready, 1)
            pool.memset(mask[0:64, SW - 64:SW], NEG).then_inc(mask_ready, 1)

            ang, hi_p, lo_p, prod, rnd, total = (rope_tmp[:, n, :] for n in range(6))
            steps = [0]

            def step(ins):
                steps[0] += 1
                ins.then_inc(angle_step, 1)
                pool.wait_ge(angle_step, steps[0])

            for n, f in enumerate(inv_freqs()):
                step(pool.memset(ang.rearrange("p (t f) -> p t f", t=TT)[:, :, n:n + 1], f))
            pool.wait_ge(pos_landed, 16)
            step(pool.tensor_copy(hi_p[:, 0:TT], pos_i[:]))
            for t in range(TT):
                half = ang[:, t * HALF:(t + 1) * HALF]
                step(pool.tensor_scalar(half, half, hi_p[:, t:t + 1], None, ALU.mult))
            step(pool.tensor_scalar(hi_p, ang, 4097.0, None, ALU.mult))
            step(pool.tensor_tensor(lo_p, hi_p, ang, ALU.subtract))
            step(pool.tensor_tensor(hi_p, hi_p, lo_p, ALU.subtract))
            step(pool.tensor_tensor(lo_p, ang, hi_p, ALU.subtract))
            step(pool.memset(total, 0.0))
            for part in (hi_p, lo_p):
                for n, piece in enumerate(turn_pieces(5)):
                    step(pool.tensor_scalar(prod, part, piece, None, ALU.mult))
                    for _ in range(2 if n == 0 else 1):
                        step(pool.tensor_scalar(rnd, prod, MAGIC, None, ALU.add))
                        step(pool.tensor_scalar(rnd, rnd, MAGIC, None, ALU.subtract))
                        step(pool.tensor_tensor(prod, prod, rnd, ALU.subtract))
                    step(pool.tensor_tensor(total, total, prod, ALU.add))
            step(pool.tensor_scalar(prod, total, 0.25, None, ALU.add))
            for n, angle in enumerate((prod, total)):
                step(pool.tensor_scalar(rnd, angle, MAGIC, None, ALU.add))
                step(pool.tensor_scalar(rnd, rnd, MAGIC, None, ALU.subtract))
                pool.tensor_tensor(rope_cs[:, n, :, :].rearrange("p t f -> p (t f)"), angle, rnd, ALU.subtract).then_inc(angle_ready, 1)
                pool.wait_ge(angle_ready, n + 1)

            def products(x1, x2, h, s):
                for n, (v, c) in enumerate(((x1, 0), (x2, 1), (x2, 0), (x1, 1))):
                    pool.tensor_tensor(rot[:, n, h, :, :], v, rope_cs[:, c, :, :], ALU.mult).then_inc(s, 1)

            def sums(x1, x2, h, s):
                pool.tensor_tensor(x1, rot[:, 0, h, :, :], rot[:, 1, h, :, :], ALU.subtract).then_inc(s, 1)
                pool.tensor_tensor(x2, rot[:, 2, h, :, :], rot[:, 3, h, :, :], ALU.add).then_inc(s, 1)

            pool.wait_ge(rope_ready, 1)
            pool.wait_ge(kpe_ready, 1)
            products(kpe_row[:, :, 0:HALF], kpe_row[:, :, HALF:ROPE], 0, kpe_prod)
            pool.wait_ge(kpe_prod, 4)
            sums(kpe_rot[:, :, 0:HALF], kpe_rot[:, :, HALF:ROPE], 0, kpe_rotated)
            pool.wait_ge(kpe_rotated, 2)

            with pool.Fori(0, PAIRS) as j:
                pool.wait_ge(q_ready, j + 1)
                pe_cols = [h * (NOPE + ROPE) + NOPE for h in range(2)]
                for h, a in enumerate(pe_cols):
                    products(q_row[:, :, a:a + HALF], q_row[:, :, a + HALF:a + ROPE], h, q_prod)
                pool.wait_ge(q_prod, j * 8 + 8)
                for h, a in enumerate(pe_cols):
                    sums(q_row[:, :, a:a + HALF], q_row[:, :, a + HALF:a + ROPE], h, q_rotated)
                pool.wait_ge(q_rotated, j * 4 + 4)

            pool.wait_ge(o_ready, PAIRS)
            pool.wait_ge(chunk_out, N_MLA)
            for c in range(CH):
                if c >= 2:
                    pool.wait_ge(turned, 2 * (T_MEM + c - 1))
                    pool.wait_ge(ss_ready, SS_KV + TT * (c - 1))
                pool.dma_start(rows[:, c % 2, :, :], mem_v[:, :, NC * c:NC * (c + 1)]).then_inc(mem_landed[c % 2], 16)
            pool.wait_ge(conv_step, KT * CONV_STEPS + 1)
            pool.memset(mean_w[:], 1.0 / D).then_inc(mean_ready, 1)
            pool.wait_ge(chunk_out, N_WOUT)
            pool.dma_start(fin_g[:], final_norm_g.rearrange("(o n) -> o n", o=1).to_broadcast([P, D])).then_inc(fin_landed, 16)

        @block.scalar
        def _(act):
            def hi(u, r=0):
                s = u % RING
                act.wait_ge(landed[s], 16 * (u // RING + 1) + r * (16 // RING))
                wait(act, used, u - RING + 1 + r)
                act.activation(whi[:, s, :], raw[:, s, :], ACT.Copy).then_inc(hi_ready, 1)

            def turn_out(turn, dst, k0, gain=None, banks=(0, 1)):
                for b in banks:
                    act.wait_ge(turned, turn * 2 + (b + 1))
                    if gain is None:
                        last = act.activation(dst[:, ds(k0 + 2 * b, 2), :], bank_blocks(b), ACT.Copy)
                    else:
                        for k in (2 * b, 2 * b + 1):
                            last = act.activation(dst[:, k0 + k, :], ps[:, 6 + b, SEQ * (k % 2):SEQ * (k % 2 + 1)], ACT.Copy,
                                                  scale=vec[:, gain + k0 + k:gain + k0 + k + 1])
                    last.then_inc(turn_hi, 1)

            def bank_blocks(b):
                return ps[:, 6 + b, :].rearrange("p (k s) -> p k s", k=2)

            def square_sums(scratch, src, to):
                for t in range(TT):
                    act.activation(scratch[:, t, :], src[:, t, :], ACT.Square, accum_out=to[:, t:t + 1]).then_inc(ss_ready, 1)

            def chunk_squares(scratch, src, c, done):
                act.wait_ge(ss_ready, done)
                for t in range(TT):
                    act.activation(scratch[:, t, :], src[:, t, :], ACT.Square, accum_out=ss_part[:, t, c:c + 1]).then_inc(ss_ready, 1)

            def root(dst, src, width):
                act.activation(dst, src, ACT.Sqrt, bias=eps, scale=1.0 / width).then_inc(sd_ready, 1)

            def glu_gate():
                for t in range(TT):
                    last = act.activation(rows[:, 1, t, :], ps[:, 2 + t, :], ACT.Sigmoid, scale=rs_x[:, t:t + 1])
                last.then_inc(sg_ready, 1)

            def scaled_rows(dst, bank, width, scale, done):
                for t in range(TT):
                    last = act.activation(dst[:, t, :], ps[:, bank + t, 0:width], ACT.Copy, scale=scale[:, t:t + 1])
                last.then_inc(done, 1)

            act.dma_start(vec_rows[0:KT, :], norm_mix_g.rearrange("o (k p) -> (o k) p", p=P)).then_inc(mix_landed, 16)
            act.wait_ge(consts, 3)
            act.activation(stat[:, 1:2], eps, ACT.Copy)
            act.wait_ge(vec_ready, 1)
            turn_out(T_X, a_hi, 0, V_MIX, [0])
            for k in range(UPC):
                hi(U_CONV + k)
                if k == 0:
                    turn_out(T_X, a_hi, 0, V_MIX, [1])
                if k in X_AFTER:
                    c = X_AFTER.index(k) + 1
                    turn_out(T_X + c, a_hi, CPB * c, V_MIX)
            square_sums(sq_x, x_in, ss_x)
            hi(8)
            act.wait_ge(ss_ready, SS_X)
            root(sd_x, ss_x, D)
            for k in range(6, 2 * UPC):
                hi(U_CONV + k + LEAD)
                if k == 9:
                    act.wait_ge(used, U_CONV + UPC)
                    act.wait_ge(rs_ready, R_X)
                    glu_gate()
                if k == 12:
                    act.wait_ge(angle_ready, 2)
                    cs = rope_cs[:].rearrange("p c t f -> p (c t f)")
                    act.activation(cs, cs, ACT.Sin, scale=TWO_PI).then_inc(rope_ready, 1)
            act.wait_ge(consts, 4)
            with act.Fori(1, CH) as i:
                r = i * (2 * UPC)
                for k in range(2 * UPC):
                    hi(U_CONV + k + LEAD, r)
                    if k == 2:
                        turn_out(i + (T_CONV - 1), hconv[:, :, PAD:], i * 4 - 4)
                    if k == 8:
                        act.wait_ge(used, r + (U_CONV + UPC))
                        act.wait_ge(chunk_out, i)
                        glu_gate()

            for k in range(UPC):
                hi(U_CQ + k + LEAD)
                if k == 2:
                    turn_out(T_CONV + CH - 1, hconv[:, :, PAD:], 4 * (CH - 1))
            act.wait_ge(used, U_CQ + UPC)
            scaled_rows(rows[:, 0, :, :], 2, LORA, rs_x, chunk_out)
            act.wait_ge(chunk_out, N_CQ + 1)
            square_sums(sq_lat, rows[:, 0, :, :], ss_q)
            act.wait_ge(ss_ready, SS_Q)
            root(sd_q, ss_q, LORA)
            hi(U_KPE + LEAD)
            act.wait_ge(vec_ready, 2)
            for k in range(UPC):
                hi(U_CKV + k + LEAD)
                if k == 0:
                    act.wait_ge(used, U_KPE + 1)
                    act.activation(kpe_sum[:], ps[0:ROPE, 4, 0:SEQ], ACT.Copy).then_inc(kpe_out, 1)
                if k == 1:
                    act.wait_ge(kpe_turned, 1)
                    for t in range(TT):
                        last = act.activation(kpe_row[:, t, :], ps[:, 5, ROPE * t:ROPE * (t + 1)], ACT.Copy, scale=rs_x[:, t:t + 1])
                    last.then_inc(kpe_ready, 1)
                if k == 2:
                    turn_out(T_CQ, cq_hi, 0, V_QG)
                if k == 5:
                    act.wait_ge(kpe_turned, 2)
                    act.activation(kpeT[:], ps[0:ROPE, 5, 0:SEQ], ACT.Copy).then_inc(kpeT_ready, 1)
            act.wait_ge(used, U_CKV + UPC)
            scaled_rows(rows[:, 1, :, :], 0, LORA, rs_x, chunk_out)
            turn_out(T_CKV, ckv_hi, 0, V_KG)
            act.wait_ge(chunk_out, N_CKV + 1)
            act.wait_ge(ss_ready, SS_Q)
            square_sums(sq_lat, rows[:, 1, :, :], ss_kv)
            act.wait_ge(ss_ready, SS_KV)
            root(sd_kv, ss_kv, LORA)

            with act.Fori(0, PAIRS) as j:
                r = j * ATT_UNITS
                for k in range(ATT_UNITS):
                    hi(U_ATT + k + LEAD, r)
                    if k == 3:
                        act.wait_ge(used, r + (U_ATT + 4))
                        act.wait_ge(rs_ready, R_KV)
                        scaled_rows(q_row, 2, QW, rs_q, q_ready)
                        scaled_rows(kv_row, 4, KVW, rs_kv, kv_ready)
                    if k == 5:
                        act.wait_ge(qk_turned, j * 3 + 1)
                        act.activation(qT[:].rearrange("p h s -> p (h s)"), ps[:, 6, :], ACT.Copy).then_inc(qT_ready, 1)
                        act.wait_ge(qk_turned, j * 3 + 2)
                        act.activation(kT[:].rearrange("p h s -> p (h s)"), ps[:, 7, :], ACT.Copy).then_inc(kT_ready, 1)
                        act.wait_ge(qk_turned, j * 3 + 3)
                        act.activation(qrT[:].rearrange("p h s -> p (h s)"), ps[0:ROPE, 2, :], ACT.Copy).then_inc(qT_ready, 1)
                    if k == 7:
                        act.wait_ge(ntop_ready, j + 1)
                        for n, (h, a, b) in enumerate(SCORES):
                            act.activation(probs[:, h, a:b], probs[:, h, a:b], ACT.Exp, bias=ntop[:, n:n + 1], scale=SM,
                                           accum_out=den[:, n:n + 1]).then_inc(exp_ready, 1)
                    if k == 9:
                        act.wait_ge(p_turned, j * 2 + 1)
                        act.activation(pT[:, 0, :], ps[:, 5, 0:SW], ACT.Copy).then_inc(pT_ready, 1)
                        act.wait_ge(p_turned, j * 2 + 2)
                        act.activation(pT[:, 1, :], ps[:, 6, 0:SW], ACT.Copy).then_inc(pT_ready, 1)
                    if k == 10:
                        act.wait_ge(o_ready, j + 1)
                        act.activation(c_hi[:, ds(j * 2, 2), :], ps[:, 7, :].rearrange("p (k s) -> p k s", k=2), ACT.Copy).then_inc(o_hi, 1)

            for c in range(CH):
                for k in range(UPC):
                    hi(U_MLA + UPC * c + k + LEAD)
                    if k == 2:
                        act.wait_ge(mem_landed[c % 2], 16 * (c // 2 + 1))
                        chunk_squares(sq_mem, rows[:, c % 2, :, :], c, SS_KV + TT * c)
                        turn_out(T_MEM + c, m_hi, 4 * c, V_MEMN)
                    if k == 4:
                        act.wait_ge(chunk_out, N_MLA)
                        for half in (D, 0):
                            g = gates[:, :, half + NC * c:half + NC * (c + 1)]
                            act.activation(g, g, ACT.Sigmoid).then_inc(gate_ready, 1)
            act.wait_ge(sum_ready, 1)
            root(sd_n, ss_sum, D)

            for k in range(UPC):
                hi(U_XKV + k + LEAD)
                for m in ((0, 1, 2), (3,))[k] if k < 2 else ():
                    act.wait_ge(ln_centred, m + 1)
                    act.activation(ln_sq[:, 4 * m:4 * m + 4, :], hconv[:, 4 * m:4 * m + 4, PAD:], ACT.Square).then_inc(ln_squared, 1)
                if k == 6:
                    act.wait_ge(ln_var, 1)
                    act.activation(acc[:, 0, :], ps[:, 5, 0:SEQ], ACT.Sqrt, bias=eps).then_inc(ln_root, 1)
            act.wait_ge(used, U_XKV + UPC)
            act.wait_ge(chunk_out, N_XK)
            act.wait_ge(rs_ready, R_MEM)
            scaled_rows(rows[:, pair_of(N_XK), :, :], 2 * pair_of(N_XK), NC, rs_mem, chunk_out)
            for k in range(UPC):
                hi(U_XKV + UPC + k + LEAD)
                if 1 <= k < 5:
                    m = k - 1
                    act.wait_ge(silu_done, 4 * m + 4)
                    act.activation(a_hi[:, 4 * m:4 * m + 4, :], hconv[:, 4 * m:4 * m + 4, PAD:], ACT.Copy).then_inc(st_hi, 1)
                if k < 4:
                    act.wait_ge(ln_scaled, k + 1)
                    for n in range(4 * k, 4 * k + 4):
                        act.activation(hconv[:, n, PAD:], hconv[:, n, PAD:], ACT.Silu, bias=vec[:, V_LB + n:V_LB + n + 1],
                                       scale=vec[:, V_LG + n:V_LG + n + 1]).then_inc(silu_done, 1)
            act.wait_ge(used, U_XKV + 2 * UPC)
            scaled_rows(xv, 2 * pair_of(N_XV), NC, rs_mem, chunk_out)

            for c in range(CH):
                for k in range(UPC):
                    hi(U_COUT + UPC * c + k + LEAD)
                    if k == 3 and c == 0:
                        turn_out(T_XK, xkT, 0)
                    if k == 3 and c:
                        turn_out(T_MRG + c - 1, c_hi, 4 * (c - 1))
            for c in range(CH):
                for k in range(UPC):
                    hi(U_WOUT + UPC * c + k + LEAD)
                    if k == 3 and c == 0:
                        turn_out(T_MRG + CH - 1, c_hi, 4 * (CH - 1))
                    if k == 3 and c:
                        turn_out(T_X1 + c - 1, a_hi, 4 * (c - 1), V_NMEM)
                act.wait_ge(chunk_out, N_WOUT + c + 1)
                chunk_squares(sq_res, xres[:, :, NC * c:NC * (c + 1)], c, SS_MEM + TT * c)
            for k in range(UPC):
                hi(U_XQ + k + LEAD)
                if k == 3:
                    turn_out(T_X1 + CH - 1, a_hi, 4 * (CH - 1), V_NMEM)
                    act.wait_ge(sum_ready, 2)
                    root(sd_n, ss_sum, D)
            act.wait_ge(used, U_XQ + UPC)
            act.wait_ge(rs_ready, R_1)
            act.wait_ge(chunk_out, N_XQ)
            p = pair_of(N_XQ)
            act.activation(rows[:, p, 0, :], ps[:, 2 * p, :], ACT.Copy, scale=rs_1[:, 0:1]).then_inc(xq_row, 1)
            act.wait_ge(turned, 2 * T_XQ + 1)
            act.activation(xqT[:, 0:2, :], bank_blocks(0), ACT.Copy).then_inc(turn_hi, 1)
            for h in range(XH):
                act.wait_ge(x_ntop, h + 1)
                for t in range(TT):
                    n = TT * h + t
                    act.activation(xp[:, h, t, :], ps[:, h, SEQ * t:SEQ * (t + 1)], ACT.Exp, bias=xntop[:, n:n + 1], scale=XSM,
                                   accum_out=xden[:, n:n + 1]).then_inc(x_exp, 1)
            for h in range(XH):
                act.wait_ge(x_pturned, h + 1)
                act.activation(xpT[:, h, :, :], ps[:, 4 + h, :].rearrange("p (k s) -> p k s", k=2), ACT.Copy).then_inc(x_pT, 1)
            for b in range(2):
                act.wait_ge(x_o, b + 1)
                act.activation(xo_hi[:, 2 * b:2 * b + 2, :], ps[:, b, :].rearrange("p (k s) -> p k s", k=2), ACT.Copy).then_inc(x_ohi, 1)
            def x2_squares(c):
                act.wait_ge(chunk_out, N_XO + c + 1)
                chunk_squares(sq_res, xres[:, :, NC * c:NC * (c + 1)], c, SS_1 + TT * c)

            for c in range(CH):
                for k in range(2):
                    hi(U_XO + 2 * c + k + LEAD)
                if c:
                    turn_out(T_X2 + c - 1, a_hi, 4 * (c - 1), V_FFN)
                    x2_squares(c - 1)

            def ff_group(g, r, last, first=False):
                for c in range(CH):
                    for k in range(UPC):
                        hi(U_FF + UPC * c + k + LEAD, r)
                        if first and c == 0 and k == 1:
                            turn_out(T_X2 + CH - 1, a_hi, 4 * (CH - 1), V_FFN)
                        if first and c == 0 and k == 2:
                            x2_squares(CH - 1)
                        if first and c == 0 and k == 4:
                            act.wait_ge(sum_ready, 3)
                            root(sd_n, ss_sum, D)
                        if k == 3 and c:
                            turn_out(g * CH + (T_FF + c - 1), c_hi, 4 * (c - 1))
                    act.wait_ge(used, r + (U_FF + UPC * (c + 1)))
                    act.wait_ge(rs_ready, R_2)
                    scaled_relu(c)
                for c in range(CH):
                    for k in range(UPC):
                        if not last or UPC * (CH + c) + k + LEAD < FF_UNITS:
                            hi(U_FF + UPC * (CH + c) + k + LEAD, r)
                        if k == 3 and c == 0:
                            turn_out(g * CH + (T_FF + CH - 1), c_hi, 4 * (CH - 1))
                    if last and c < CH - 1:
                        act.wait_ge(chunk_out, N_FF + g * 2 * CH + CH + c + 1)
                        chunk_squares(sq_res, xres[:, :, NC * c:NC * (c + 1)], c, SS_2 + TT * c)

            def scaled_relu(c):
                p = pair_of(N_FF + c)
                for t in range(TT):
                    last = act.activation(rows[:, p, t, :], ps[:, 2 * p + t, :], ACT.Relu, scale=rs_2[:, t:t + 1])
                last.then_inc(relu_ready, 1)

            ff_group(0, 0, False, True)
            with act.Fori(1, GROUPS - 1) as g:
                ff_group(g, g * FF_UNITS, False)
            ff_group(GROUPS - 1, (GROUPS - 1) * FF_UNITS, True)
            act.wait_ge(ss_ready, SS_3 - TT)
            for t in range(TT):
                act.wait_ge(last_rows, t + 1)
                act.activation(sq_res[:, t, :], xres[:, t, D - NC:], ACT.Square, accum_out=ss_part[:, t, CH - 1:CH]).then_inc(ss_ready, 1)
            act.wait_ge(sum_ready, 4)
            root(sd_n, ss_sum, D)
            act.wait_ge(rs_ready, R_3)
            for c in range(2):
                act.wait_ge(fin_gained, c + 1)
                for t in range(TT):
                    cols = fin[:, t, NC * c:NC * (c + 1)]
                    last = act.activation(cols, cols, ACT.Copy, scale=rs_3[:, t:t + 1])
                last.then_inc(fin_act, 1)

        @block.vector
        def _(dve):
            def lo(u, r=0):
                s = u % RING
                dve.wait_ge(hi_ready, u + 1 + r)
                dve.tensor_tensor(wlo[:, s, :], raw[:, s, :], whi[:, s, :].bitcast(F32), ALU.subtract).then_inc(lo_ready, 1)

            def bank_blocks(b):
                return ps[:, 6 + b, :].rearrange("p (k s) -> p k s", k=2)

            def turn_low(turn, dst_lo, dst_hi, k0, gain=None, banks=(0, 1)):
                for b in banks:
                    dve.wait_ge(turn_hi, turn * 2 + (b + 1))
                    if gain is None:
                        last = dve.tensor_tensor(dst_lo[:, k0 + 2 * b:k0 + 2 * b + 2, :], bank_blocks(b),
                                                 dst_hi[:, k0 + 2 * b:k0 + 2 * b + 2, :].bitcast(F32), ALU.subtract)
                    else:
                        for k in (2 * b, 2 * b + 1):
                            g = gain + k0 + k
                            last = dve.scalar_tensor_tensor(out=dst_lo[:, k0 + k, :], in0=ps[:, 6 + b, SEQ * (k % 2):SEQ * (k % 2 + 1)],
                                                            scalar=vec[:, g:g + 1], in1=dst_hi[:, k0 + k, :].bitcast(F32),
                                                            op0=ALU.mult, op1=ALU.subtract)
                    last.then_inc(turn_lo, 1)

            def reciprocal(dst, src, n):
                dve.wait_ge(sd_ready, n)
                dve.reciprocal(dst, src).then_inc(rs_ready, 1)

            def add_parts(squares, n):
                dve.wait_ge(ss_ready, squares)
                dve.tensor_reduce(ss_sum, ss_part, AX_X, ALU.add).then_inc(sum_ready, 1)

            def glu():
                for t in range(TT):
                    last = dve.scalar_tensor_tensor(out=rows[:, 0, t, :], in0=ps[:, t, :], scalar=rs_x[:, t:t + 1],
                                                    in1=rows[:, 1, t, :], op0=ALU.mult, op1=ALU.mult)
                last.then_inc(chunk_out, 1)

            def conv(kt, steps):
                for n in steps:
                    h = hconv[:, ds(kt, 1), :].rearrange("p k s -> p (k s)")
                    tap = n - 1
                    in_turn = n in (0, 1, CONV_STEPS - 1)
                    dve.wait_ge(conv_step, kt * CONV_STEPS + (n + 1 if in_turn else n))
                    to = acc[:, tap % 2, :]
                    if n == 0:
                        ins = dve.tensor_copy(cwk[:], cw[:, ds(kt, 1), :].rearrange("p k s -> p (k s)"))
                    elif n == CONV_STEPS - 1:
                        ins = dve.tensor_tensor(h[:, PAD:HC], acc[:, 0, :], acc[:, 1, :], ALU.add)
                    elif tap == 0:
                        ins = dve.tensor_scalar(to, h[:, 0:SEQ], cwk[:, 0:1], cwk[:, CONV_K:CONV_K + 1], ALU.mult, ALU.add)
                    elif tap == 1:
                        ins = dve.tensor_scalar(to, h[:, 1:1 + SEQ], cwk[:, 1:2], None, ALU.mult)
                    else:
                        ins = dve.scalar_tensor_tensor(out=to, in0=h[:, tap:tap + SEQ], scalar=cwk[:, tap:tap + 1], in1=to,
                                                       op0=ALU.mult, op1=ALU.add)
                    ins.then_inc(conv_step, 1)

            def share(k, parts):
                return range(CONV_STEPS * k // parts, CONV_STEPS * (k + 1) // parts)

            def conv_run(first, tiles, k, parts):
                for n in range(tiles * CONV_STEPS * k // parts, tiles * CONV_STEPS * (k + 1) // parts):
                    conv(first + n // CONV_STEPS, [n % CONV_STEPS])

            dve.wait_ge(vec_turned, 1)
            dve.tensor_copy(vec[:, 0:KT], ps[:, 5, 0:KT]).then_inc(vec_ready, 1)
            dve.wait_ge(vec_ready, 1)
            turn_low(T_X, a_lo, a_hi, 0, V_MIX, [0])
            for k in range(UPC):
                lo(U_CONV + k)
                if k == 0:
                    turn_low(T_X, a_lo, a_hi, 0, V_MIX, [1])
                if k in X_AFTER:
                    c = X_AFTER.index(k) + 1
                    turn_low(T_X + c, a_lo, a_hi, CPB * c, V_MIX)
            lo(8)
            for k in range(6, 2 * UPC):
                lo(U_CONV + k + LEAD)
                if k == 8:
                    reciprocal(rs_x, sd_x, R_X)
                if k == 10:
                    dve.wait_ge(vec_turned, 2)
                    dve.tensor_copy(vec[:, KT:], ps[:, 5, KT:V_N]).then_inc(vec_ready, 1)
                    dve.wait_ge(cw_turned, 1)
                    dve.tensor_copy(cw[:].rearrange("p k s -> p (k s)"), ps[:, 4, :]).then_inc(conv_step, 1)
            dve.wait_ge(used, U_CONV + 2 * UPC)
            dve.wait_ge(sg_ready, 1)
            dve.wait_ge(rs_ready, R_X)
            glu()
            spots = 2 * UPC * (CH - 1) - 4
            for i in range(1, CH):
                u = U_CONV + 2 * UPC * i
                for k in range(2 * UPC):
                    lo(u + k + LEAD)
                    if (i, k) == (1, 4):
                        dve.wait_ge(turn_hi, 2 * (T_CONV + 1))
                    spot = 2 * UPC * (i - 1) + k - 4
                    if spot >= 0:
                        conv_run(0, CONV_A, spot, spots)
                dve.wait_ge(used, u + 2 * UPC)
                dve.wait_ge(sg_ready, i + 1)
                glu()

            dve.wait_ge(turn_hi, 2 * (T_CONV + 2))
            for k in range(UPC):
                lo(U_CQ + k + LEAD)
                conv_run(CONV_A, CONV_B, k, 2 * UPC)
            reciprocal(rs_q, sd_q, R_Q)
            lo(U_KPE + LEAD)
            dve.wait_ge(vec_ready, 2)
            for k in range(UPC):
                lo(U_CKV + k + LEAD)
                if k == 2:
                    turn_low(T_CQ, cq_lo, cq_hi, 0, V_QG)
                conv_run(CONV_A, CONV_B, UPC + k, 2 * UPC)
            turn_low(T_CKV, ckv_lo, ckv_hi, 0, V_KG)
            reciprocal(rs_kv, sd_kv, R_KV)

            dve.wait_ge(mask_ready, 3)
            dve.wait_ge(turn_hi, 2 * (T_CONV + CH))
            CONV_AT = (0, 1, 2, 4, 5, 6, 7, 8, 9, 10)
            with dve.Fori(0, PAIRS) as j:
                r = j * ATT_UNITS
                for k in range(ATT_UNITS):
                    lo(U_ATT + k + LEAD, r)
                    if k == 6:
                        dve.wait_ge(scored, j * 2 + 2)
                        conv(j + (CONV_A + CONV_B), share(CONV_AT.index(k), len(CONV_AT)))
                        for n, (h, a, b) in enumerate(SCORES):
                            dve.tensor_tensor_reduce(probs[:, h, a:b], ps[:, 3 + h, a:b], mask[:, a:b], 1.0, NEG, ALU.add, ALU.max,
                                                     top[:, n:n + 1]).then_inc(masked, 1)
                        dve.wait_ge(masked, j * 4 + 4)
                        dve.tensor_scalar(ntop, top, -SM, None, ALU.mult).then_inc(ntop_ready, 1)
                    if k == 8:
                        dve.wait_ge(exp_ready, j * 4 + 4)
                        dve.reciprocal(rden, den).then_inc(rden_ready, 1)
                        dve.wait_ge(rden_ready, j + 1)
                        for n, (h, a, b) in enumerate(SCORES):
                            dve.tensor_scalar(probs[:, h, a:b], probs[:, h, a:b], rden[:, n:n + 1], None, ALU.mult).then_inc(probs_ready, 1)
                    if k == 10:
                        dve.wait_ge(o_hi, j + 1)
                        dve.tensor_tensor(c_lo[:, ds(j * 2, 2), :], ps[:, 7, :].rearrange("p (k s) -> p k s", k=2),
                                          c_hi[:, ds(j * 2, 2), :].bitcast(F32), ALU.subtract).then_inc(o_lo, 1)
                    if k in CONV_AT and k != 6:
                        conv(j + (CONV_A + CONV_B), share(CONV_AT.index(k), len(CONV_AT)))
                dve.wait_ge(used, r + (U_ATT + ATT_UNITS))
                dve.wait_ge(bias_landed, j * 16 + 16)
                for t in range(TT):
                    last = dve.scalar_tensor_tensor(out=gates[:, t, ds(j * NC, NC)], in0=ps[:, t, :], scalar=rs_x[:, t:t + 1],
                                                    in1=gbias[:], op0=ALU.mult, op1=ALU.add)
                last.then_inc(chunk_out, 1)

            def ln_tree(src, first):
                adds = ((ln_sum[:, 0:4, :], src[:, 0:4, :], src[:, 8:12, :]), (ln_sum[:, 4:8, :], src[:, 4:8, :], src[:, 12:16, :]),
                        (ln_sum[:, 0:4, :], ln_sum[:, 0:4, :], ln_sum[:, 4:8, :]),
                        (ln_sum[:, 0:2, :], ln_sum[:, 0:2, :], ln_sum[:, 2:4, :]),
                        (ln_sum[:, 0:1, :], ln_sum[:, 0:1, :], ln_sum[:, 1:2, :]))
                return adds

            def ln_add(src, first, n):
                to, a, b = ln_tree(src, first)[n]
                if n >= 2:
                    dve.wait_ge(ln_added, first + n)
                dve.tensor_tensor(to, a, b, ALU.add).then_inc(ln_added, 1)

            def spread(v):
                return v.rearrange("p (k s) -> p k s", k=1).to_broadcast([P, 4, SEQ])

            def centre(m):
                dve.wait_ge(ln_mean, 1)
                dve.tensor_tensor(y[:, 4 * m:4 * m + 4, :], y[:, 4 * m:4 * m + 4, :], spread(ps[:, 4, 0:SEQ]), ALU.subtract).then_inc(ln_centred, 1)

            def scale_by_root(m):
                dve.tensor_tensor(y[:, 4 * m:4 * m + 4, :], y[:, 4 * m:4 * m + 4, :], spread(acc[:, 0, :]), ALU.mult).then_inc(ln_scaled, 1)

            y = hconv[:, :, PAD:]
            for c in range(CH):
                for k in range(UPC):
                    lo(U_MLA + UPC * c + k + LEAD)
                    if k == 2:
                        turn_low(T_MEM + c, m_lo, m_hi, 4 * c, V_MEMN)
                    if c < CH - 1:
                        conv_run(CONV_A + CONV_B + PAIRS, CONV_D, UPC * c + k, UPC * (CH - 1))
                    elif k < 4:
                        if k == 0:
                            dve.wait_ge(conv_step, KT * CONV_STEPS + 1)
                        ln_add(y, 0, k)
                        if k == 3:
                            ln_add(y, 0, 4)
                    elif k == 4:
                        add_parts(SS_MEM, 1)
                    else:
                        centre(k - 5)
                n = N_MLA + c
                dve.wait_ge(used, U_MLA + UPC * (c + 1))
                dve.wait_ge(gate_ready, 2 * c + 1)
                g = gates[:, :, D + NC * c:D + NC * (c + 1)]
                dve.tensor_tensor(g, ps[:, 2 * pair_of(n):2 * pair_of(n) + 2, :], g, ALU.mult).then_inc(chunk_out, 1)

            for k in range(UPC):
                lo(U_XKV + k + LEAD)
                if k == 0:
                    centre(3)
                if k == 1:
                    reciprocal(rs_mem, sd_n, R_MEM)
                if k in (1, 2):
                    dve.wait_ge(ln_squared, k + 2)
                    ln_add(ln_sq, 5, k - 1)
                if k == 3:
                    for n in (2, 3, 4):
                        ln_add(ln_sq, 5, n)
                if k == 7:
                    dve.wait_ge(ln_root, 1)
                    dve.reciprocal(acc[:, 0, :], acc[:, 0, :]).then_inc(ln_root, 1)
                    dve.wait_ge(ln_root, 2)
                    scale_by_root(0)
            for k in range(UPC):
                lo(U_XKV + UPC + k + LEAD)
                if k < 3:
                    scale_by_root(k + 1)
                if 2 <= k < 6:
                    m = k - 2
                    dve.wait_ge(st_hi, m + 1)
                    dve.tensor_tensor(a_lo[:, 4 * m:4 * m + 4, :], y[:, 4 * m:4 * m + 4, :], a_hi[:, 4 * m:4 * m + 4, :].bitcast(F32),
                                      ALU.subtract).then_inc(st_lo, 1)

            for c in range(CH):
                for k in range(UPC):
                    lo(U_COUT + UPC * c + k + LEAD)
                    if k == 3 and c:
                        turn_low(T_MRG + c - 1, c_lo, c_hi, 4 * (c - 1))
                n = N_COUT + c
                p = pair_of(n)
                dve.wait_ge(used, U_COUT + UPC * (c + 1))
                dve.wait_ge(chunk_out, n)
                cols = slice(NC * c, NC * (c + 1))
                dve.tensor_tensor(rows[:, p, :, :], ps[:, 2 * p:2 * p + 2, :], gates[:, :, cols], ALU.mult).then_inc(gated, 1)
                dve.wait_ge(gated, c + 1)
                dve.tensor_tensor(rows[:, p, :, :], rows[:, p, :, :], gates[:, :, D + NC * c:D + NC * (c + 1)], ALU.add).then_inc(chunk_out, 1)

            def add_to_residual(n, c):
                p = pair_of(n)
                cols = xres[:, :, NC * c:NC * (c + 1)]
                dve.tensor_tensor(cols, ps[:, 2 * p:2 * p + 2, :], cols, ALU.add).then_inc(chunk_out, 1)

            for c in range(CH):
                for k in range(UPC):
                    lo(U_WOUT + UPC * c + k + LEAD)
                    if k == 3 and c == 0:
                        turn_low(T_MRG + CH - 1, c_lo, c_hi, 4 * (CH - 1))
                    if k == 3 and c:
                        turn_low(T_X1 + c - 1, a_lo, a_hi, 4 * (c - 1), V_NMEM)
                dve.wait_ge(used, U_WOUT + UPC * (c + 1))
                dve.wait_ge(res_landed, 16)
                add_to_residual(N_WOUT + c, c)
            for k in range(UPC):
                lo(U_XQ + k + LEAD)
                if k == 1:
                    add_parts(SS_1, 2)
                if k == 3:
                    turn_low(T_X1 + CH - 1, a_lo, a_hi, 4 * (CH - 1), V_NMEM)
                if k == 5:
                    reciprocal(rs_1, sd_n, R_1)
            p = pair_of(N_XQ)
            dve.wait_ge(used, U_XQ + UPC)
            dve.wait_ge(rs_ready, R_1)
            dve.tensor_scalar(rows[:, p, 1, :], ps[:, 2 * p + 1, :], rs_1[:, 1:2], None, ALU.mult).then_inc(chunk_out, 1)
            dve.wait_ge(turned, 2 * T_XQ + 2)
            dve.tensor_copy(xqT[:, 2:4, :], bank_blocks(1)).then_inc(turn_hi, 1)
            for h in range(XH):
                dve.wait_ge(x_scored, h + 1)
                dve.tensor_reduce(xtop[:, TT * h:TT * (h + 1)], ps[:, h, :].rearrange("p (t m) -> p t m", t=TT), AX_X, ALU.max).then_inc(x_top, 1)
                dve.wait_ge(x_top, h + 1)
                dve.tensor_scalar(xntop[:, TT * h:TT * (h + 1)], xtop[:, TT * h:TT * (h + 1)], -XSM, None, ALU.mult).then_inc(x_ntop, 1)
            for h in range(XH):
                dve.wait_ge(x_exp, TT * (h + 1))
                dve.reciprocal(xrden[:, TT * h:TT * (h + 1)], xden[:, TT * h:TT * (h + 1)]).then_inc(x_rden, 1)
                dve.wait_ge(x_rden, h + 1)
                for t in range(TT):
                    n = TT * h + t
                    dve.tensor_scalar(xp[:, h, t, :], xp[:, h, t, :], xrden[:, n:n + 1], None, ALU.mult).then_inc(x_probs, 1)
            for b in range(2):
                dve.wait_ge(x_ohi, b + 1)
                dve.tensor_tensor(xo_lo[:, 2 * b:2 * b + 2, :], ps[:, b, :].rearrange("p (k s) -> p k s", k=2),
                                  xo_hi[:, 2 * b:2 * b + 2, :].bitcast(F32), ALU.subtract).then_inc(x_olo, 1)
            for c in range(CH):
                for k in range(2):
                    lo(U_XO + 2 * c + k + LEAD)
                if c:
                    turn_low(T_X2 + c - 1, a_lo, a_hi, 4 * (c - 1), V_FFN)
                dve.wait_ge(used, U_XO + 2 * (c + 1))
                add_to_residual(N_XO + c, c)

            def gain(c):
                if c == 0:
                    dve.wait_ge(fin_landed, 16)
                dve.wait_ge(chunk_out, N_FF + GROUPS * 2 * CH - CH + c + 1)
                cols = slice(NC * c, NC * (c + 1))
                for t in range(TT):
                    last = dve.tensor_tensor(fin[:, t, cols], xres[:, t, cols], fin_g[:, cols], ALU.mult)
                last.then_inc(fin_gained, 1)

            def ff_group(g, r, last, first=False):
                for c in range(CH):
                    for k in range(UPC):
                        lo(U_FF + UPC * c + k + LEAD, r)
                        if first and c == 0 and k == 1:
                            turn_low(T_X2 + CH - 1, a_lo, a_hi, 4 * (CH - 1), V_FFN)
                        if first and c == 0 and k == 4:
                            add_parts(SS_2, 3)
                            reciprocal(rs_2, sd_n, R_2)
                        if k == 3 and c:
                            turn_low(g * CH + (T_FF + c - 1), c_lo, c_hi, 4 * (c - 1))
                    p = pair_of(N_FF + c)
                    dve.wait_ge(relu_ready, g * CH + (c + 1))
                    dve.tensor_tensor(rows[:, p, :, :], rows[:, p, :, :], rows[:, p, :, :], ALU.mult).then_inc(chunk_out, 1)
                for c in range(CH):
                    for k in range(UPC):
                        if not last or UPC * (CH + c) + k + LEAD < FF_UNITS:
                            lo(U_FF + UPC * (CH + c) + k + LEAD, r)
                        if k == 3 and c == 0:
                            turn_low(g * CH + (T_FF + CH - 1), c_lo, c_hi, 4 * (CH - 1))
                        if last and k == 4 and c:
                            gain(c - 1)
                    dve.wait_ge(used, r + (U_FF + UPC * (CH + c + 1)))
                    if last and c == CH - 1:
                        for t in range(TT):
                            cols = xres[:, t, NC * c:NC * (c + 1)]
                            dve.tensor_tensor(cols, ps[:, 2 * pair_of(N_FF + CH + c) + t, :], cols, ALU.add).then_inc(last_rows, 1)
                    else:
                        add_to_residual(N_FF + CH + c, c)

            ff_group(0, 0, False, True)
            with dve.Fori(1, GROUPS - 1) as g:
                ff_group(g, g * FF_UNITS, False)
            ff_group(GROUPS - 1, (GROUPS - 1) * FF_UNITS, True)
            add_parts(SS_3, 4)
            reciprocal(rs_3, sd_n, R_3)
            dve.wait_ge(rs_ready, R_3)
            dve.wait_ge(fin_gained, 3)
            for t in range(TT):
                cols = fin[:, t, 2 * NC:3 * NC]
                last = dve.tensor_scalar(cols, cols, rs_3[:, t:t + 1], None, ALU.mult)
            last.then_inc(fin_dve, 1)
            dve.wait_ge(last_rows, TT)
            for t in range(TT):
                cols = slice(D - NC, D)
                last = dve.scalar_tensor_tensor(out=fin[:, t, cols], in0=xres[:, t, cols], scalar=rs_3[:, t:t + 1], in1=fin_g[:, cols],
                                                op0=ALU.mult, op1=ALU.mult)
            last.then_inc(fin_dve, 1)

        @block.tensor
        def _(pe):
            def unit(u, r, x_hi, x_lo, k0, bank, first, last, kts=2, width=NC):
                s = u % RING
                pe.wait_ge(lo_ready, u + 1 + r)
                for k in range(kts):
                    for t in range(TT):
                        sum_ = ps[:, bank + t, 0:width]
                        tok = slice(P * t, P * (t + 1))
                        w_hi, w_lo = (w[:, s, width * k:width * (k + 1)] for w in (whi, wlo))
                        pe.matmul(sum_, x_hi[:, k0 + k, tok], w_hi, start=(first and k == 0), stop=False)
                        pe.matmul(sum_, x_hi[:, k0 + k, tok], w_lo, start=False, stop=False)
                        mm = pe.matmul(sum_, x_lo[:, k0 + k, tok], w_hi, start=False, stop=(last and k == kts - 1))
                mm.then_inc(used, 1)

            def turn(n, src, c0, after=None):
                for b in range(2):
                    if after is not None:
                        pe.wait_ge(after[0], after[1] + b)
                    for k in (2 * b, 2 * b + 1):
                        for t in range(TT):
                            tr = pe.transpose(ps[:, 6 + b, SEQ * (k % 2) + P * t:SEQ * (k % 2) + P * (t + 1)],
                                              src[:, t, c0 + P * k:c0 + P * (k + 1)], ident[:])
                    tr.then_inc(turned, 1)

            def split_out(n):
                return turn_lo, 2 * splits_before(n) + 1

            def copied_out(n):
                return turn_hi, n * 2 + 1

            pe.wait_ge(consts, 2)
            pe.wait_ge(mix_landed, 16)
            pe.transpose(ps[:, 5, 0:KT], vec_rows[0:KT, :], ident[0:KT, 0:KT]).then_inc(vec_turned, 1)
            pe.wait_ge(x_landed[0], 16)
            turn(T_X, x_in, 0)
            for k in range(UPC):
                if k in X_BEFORE:
                    c = X_BEFORE.index(k) + 1
                    pe.wait_ge(x_landed[c], 16)
                    turn(T_X + c, x_in, NC * c, split_out(T_X + c - 1))
                pe.wait_ge(turn_lo, k + 1)
                unit(U_CONV + k, 0, a_hi, a_lo, 2 * k, 2, k == 0, k == UPC - 1)
            pe.wait_ge(vec_landed, 16 * 7)
            pe.wait_ge(vec_ready, 1)
            pe.transpose(ps[:, 5, 0:V_N], vec_rows[0:V_N, :], ident[0:V_N, 0:V_N]).then_inc(vec_turned, 1)
            pe.wait_ge(cw_landed, 32)
            for k in range(KT):
                tr = pe.transpose(ps[:, 4, (CONV_K + 1) * k:(CONV_K + 1) * (k + 1)], cw_rows[:, P * k:P * (k + 1)],
                                  ident[0:CONV_K + 1, 0:CONV_K + 1])
            tr.then_inc(cw_turned, 1)
            for k in range(UPC):
                unit(U_CONV + UPC + k, 0, a_hi, a_lo, 2 * k, 0, k == 0, k == UPC - 1)

            with pe.Fori(1, CH) as i:
                r = i * (2 * UPC)
                pe.wait_ge(sg_ready, i)
                for k in range(UPC):
                    unit(U_CONV + k, r, a_hi, a_lo, 2 * k, 2, k == 0, k == UPC - 1)
                    if k == 2:
                        pe.wait_ge(chunk_out, i)
                        pe.wait_ge(turn_lo, 2 * CH)
                        turn(i + (T_CONV - 1), rows[:, 0, :, :], 0, (turn_hi, i * 2 + (2 * (T_CONV - 2) + 1)))
                for k in range(UPC):
                    unit(U_CONV + UPC + k, r, a_hi, a_lo, 2 * k, 0, k == 0, k == UPC - 1)

            pe.wait_ge(sg_ready, CH)
            for k in range(UPC):
                unit(U_CQ + k, 0, a_hi, a_lo, 2 * k, 2, k == 0, k == UPC - 1)
                if k == 2:
                    pe.wait_ge(chunk_out, N_CQ)
                    turn(T_CONV + CH - 1, rows[:, 0, :, :], 0, copied_out(T_CONV + CH - 2))
            pe.wait_ge(conv_step, 1)
            pe.wait_ge(lo_ready, U_KPE + 1)
            s = U_KPE % RING
            for k in range(KT):
                w_hi, w_lo = (w[:, s, ROPE * k:ROPE * (k + 1)] for w in (whi, wlo))
                pe.matmul(ps[0:ROPE, 4, 0:SEQ], w_hi, a_hi[:, k, :], start=(k == 0), stop=False)
                pe.matmul(ps[0:ROPE, 4, 0:SEQ], w_lo, a_hi[:, k, :], start=False, stop=False)
                mm = pe.matmul(ps[0:ROPE, 4, 0:SEQ], w_hi, a_lo[:, k, :], start=False, stop=(k == KT - 1))
            mm.then_inc(used, 1)
            for k in range(UPC):
                unit(U_CKV + k, 0, a_hi, a_lo, 2 * k, 0, k == 0, k == UPC - 1)
                if k == 0:
                    pe.wait_ge(kpe_out, 1)
                    pe.wait_ge(vec_ready, 2)
                    for t in range(TT):
                        tr = pe.transpose(ps[:, 5, ROPE * t:ROPE * (t + 1)], kpe_sum[:, P * t:P * (t + 1)], ident[0:ROPE, 0:ROPE])
                    tr.then_inc(kpe_turned, 1)
                if k == 2:
                    pe.wait_ge(chunk_out, N_CQ + 1)
                    turn(T_CQ, rows[:, 0, :, :], 0, copied_out(T_CQ - 1))
                if k == 4:
                    pe.wait_ge(kpe_rotated, 2)
                    for t in range(TT):
                        tr = pe.transpose(ps[0:ROPE, 5, P * t:P * (t + 1)], kpe_rot[:, t, :], ident[:])
                    tr.then_inc(kpe_turned, 1)
            pe.wait_ge(chunk_out, N_CKV + 1)
            turn(T_CKV, rows[:, 1, :, :], 0, split_out(T_CQ))
            pe.wait_ge(turn_lo, 2 * splits_before(T_CQ) + 2)
            pe.wait_ge(kpeT_ready, 1)

            with pe.Fori(0, PAIRS) as j:
                r = j * ATT_UNITS

                def gate_unit(k):
                    unit(U_ATT + 4 + k, r, a_hi, a_lo, 2 * k, 0, k == 0, k == UPC - 1)

                for n in range(2):
                    unit(U_ATT + n, r, cq_hi, cq_lo, 2 * n, 2, n == 0, n == 1, 2, QW)
                pe.wait_ge(turn_lo, 2 * splits_before(T_CKV) + 2)
                for n in range(2):
                    unit(U_ATT + 2 + n, r, ckv_hi, ckv_lo, 2 * n, 4, n == 0, n == 1)
                pe.wait_ge(chunk_out, j + N_GATE)
                gate_unit(0)
                gate_unit(1)
                pe.wait_ge(q_rotated, j * 4 + 4)
                for h in range(2):
                    a = h * (NOPE + ROPE)
                    for t in range(TT):
                        tr = pe.transpose(ps[:, 6, SEQ * h + P * t:SEQ * h + P * (t + 1)], q_row[:, t, a:a + NOPE], ident[:])
                tr.then_inc(qk_turned, 1)
                pe.wait_ge(kv_ready, j + 1)
                for h in range(2):
                    a = h * (NOPE + VD)
                    for t in range(TT):
                        tr = pe.transpose(ps[:, 7, SEQ * h + P * t:SEQ * h + P * (t + 1)], kv_row[:, t, a:a + NOPE], ident[:])
                tr.then_inc(qk_turned, 1)
                for h in range(2):
                    a = h * (NOPE + ROPE) + NOPE
                    for t in range(TT):
                        tr = pe.transpose(ps[0:ROPE, 2, SEQ * h + P * t:SEQ * h + P * (t + 1)], q_row[:, t, a:a + ROPE], ident[:])
                tr.then_inc(qk_turned, 1)
                gate_unit(2)
                pe.wait_ge(qT_ready, j * 2 + 2)
                pe.wait_ge(kT_ready, j + 1)
                for h in range(2):
                    for t in range(TT):
                        keys = P * (t + 1)
                        sc = ps[:, 3 + h, P * t:P * t + keys]
                        tok = slice(P * t, P * (t + 1))
                        pe.matmul(sc, qT[:, h, tok], kT[:, h, 0:keys], start=True, stop=False)
                        mm = pe.matmul(sc, qrT[:, h, tok], kpeT[:, 0:keys], start=False, stop=True)
                    mm.then_inc(scored, 1)
                gate_unit(3)
                gate_unit(4)
                gate_unit(5)
                for h in range(2):
                    pe.wait_ge(probs_ready, j * 4 + 2 * (h + 1))
                    for n in range(3):
                        tr = pe.transpose(ps[:, 5 + h, P * n:P * (n + 1)], probs[:, h, P * n:P * (n + 1)], ident[:])
                    tr.then_inc(p_turned, 1)
                gate_unit(6)
                pe.wait_ge(pT_ready, j * 2 + 2)
                for h in range(2):
                    a = h * (NOPE + VD) + NOPE
                    pe.matmul(ps[:, 7, SEQ * h:SEQ * (h + 1)], kv_row[:, 0, a:a + VD], pT[:, h, 0:SEQ], start=True, stop=False)
                    mm = pe.matmul(ps[:, 7, SEQ * h + P:SEQ * (h + 1)], kv_row[:, 1, a:a + VD], pT[:, h, SEQ:SW], start=False, stop=True)
                mm.then_inc(o_ready, 1)
                gate_unit(7)

            pe.wait_ge(o_lo, PAIRS)
            for c in range(CH):
                n = N_MLA + c
                if c:
                    pe.wait_ge(chunk_out, n - 1)
                for k in range(UPC):
                    unit(U_MLA + UPC * c + k, 0, c_hi, c_lo, 2 * k, 2 * pair_of(n), k == 0, k == UPC - 1)
                    if c == CH - 1 and k == 4:
                        pe.wait_ge(mean_ready, 1)
                        pe.wait_ge(ln_added, 5)
                        pe.matmul(ps[:, 4, 0:SEQ], mean_w[:], ln_sum[:, 0, :], start=True, stop=True).then_inc(ln_mean, 1)
                    if k == 2:
                        pe.wait_ge(mem_landed[c % 2], 16 * (c // 2 + 1))
                        turn(T_MEM + c, rows[:, c % 2, :, :], 0, split_out(T_MEM + c - 1) if c else None)

            for n in (N_XK, N_XV):
                u = U_XKV + UPC * (n - N_XK)
                pe.wait_ge(chunk_out, n - 1)
                for k in range(UPC):
                    if n == N_XK:
                        pe.wait_ge(turn_lo, 2 * splits_before(T_MEM) + k + 1)
                    unit(u + k, 0, m_hi, m_lo, 2 * k, 2 * pair_of(n), k == 0, k == UPC - 1)
                    if n == N_XK and k == 5:
                        pe.wait_ge(ln_added, 10)
                        pe.matmul(ps[:, 5, 0:SEQ], mean_w[:], ln_sum[:, 0, :], start=True, stop=True).then_inc(ln_var, 1)

            for c in range(CH):
                n = N_COUT + c
                pe.wait_ge(chunk_out, n - 1)
                for k in range(UPC):
                    if c == 0:
                        pe.wait_ge(st_lo, k // 2 + 1)
                    unit(U_COUT + UPC * c + k, 0, a_hi, a_lo, 2 * k, 2 * pair_of(n), k == 0, k == UPC - 1)
                    if k == 3 and c == 0:
                        turn(T_XK, rows[:, pair_of(N_XK), :, :], 0, split_out(T_XK - 1))
                    if k == 3 and c:
                        pe.wait_ge(chunk_out, n)
                        turn(T_MRG + c - 1, rows[:, pair_of(n - 1), :, :], 0, copied_out(T_XK) if c == 1 else split_out(T_MRG + c - 2))

            for c in range(CH):
                n = N_WOUT + c
                pe.wait_ge(chunk_out, n - 1)
                for k in range(UPC):
                    if c == 0:
                        pe.wait_ge(turn_lo, 2 * splits_before(T_MRG) + k + 1)
                    unit(U_WOUT + UPC * c + k, 0, c_hi, c_lo, 2 * k, 2 * pair_of(n), k == 0, k == UPC - 1)
                    if k == 3:
                        pe.wait_ge(chunk_out, n)
                        if c == 0:
                            turn(T_MRG + CH - 1, rows[:, pair_of(n - 1), :, :], 0, split_out(T_MRG + CH - 2))
                        else:
                            turn(T_X1 + c - 1, xres, NC * (c - 1), split_out(T_X1 + c - 2))

            pe.wait_ge(chunk_out, N_XQ - 1)
            for k in range(UPC):
                pe.wait_ge(turn_lo, 2 * splits_before(T_X1) + k + 1)
                unit(U_XQ + k, 0, a_hi, a_lo, 2 * k, 2 * pair_of(N_XQ), k == 0, k == UPC - 1)
                if k == 3:
                    pe.wait_ge(chunk_out, N_XQ)
                    turn(T_X1 + CH - 1, xres, NC * (CH - 1), split_out(T_X1 + CH - 2))
            pe.wait_ge(xq_row, 1)
            pe.wait_ge(chunk_out, N_XQ + 1)
            turn(T_XQ, rows[:, pair_of(N_XQ), :, :], 0, split_out(T_XQ - 1))
            pe.wait_ge(turn_hi, 2 * T_XQ + 2)
            for h in range(XH):
                for t in range(TT):
                    mm = pe.matmul(ps[:, h, SEQ * t:SEQ * (t + 1)], xqT[:, h, P * t:P * (t + 1)], xkT[:, h, :], start=True, stop=True)
                mm.then_inc(x_scored, 1)
            for h in range(XH):
                pe.wait_ge(x_probs, TT * (h + 1))
                for k in range(TT):
                    for t in range(TT):
                        tr = pe.transpose(ps[:, 4 + h, SEQ * k + P * t:SEQ * k + P * (t + 1)], xp[:, h, t, P * k:P * (k + 1)], ident[:])
                tr.then_inc(x_pturned, 1)
            for h in range(XH):
                pe.wait_ge(x_pT, h + 1)
                for k in range(TT):
                    mm = pe.matmul(ps[:, h // 2, SEQ * (h % 2):SEQ * (h % 2 + 1)], xv[:, k, P * h:P * (h + 1)], xpT[:, h, k, :],
                                   start=(k == 0), stop=(k == TT - 1))
                if h % 2:
                    mm.then_inc(x_o, 1)
            pe.wait_ge(x_olo, 2)
            for c in range(CH):
                n = N_XO + c
                pe.wait_ge(chunk_out, n - 1)
                for k in range(2):
                    unit(U_XO + 2 * c + k, 0, xo_hi, xo_lo, 2 * k, 2 * pair_of(n), k == 0, k == 1)
                if c:
                    pe.wait_ge(chunk_out, n)
                    turn(T_X2 + c - 1, xres, NC * (c - 1), split_out(T_X2 + c - 2) if c > 1 else None)

            def ff_group(g, r, first=False):
                for c in range(2 * CH):
                    n = N_FF + c
                    p = pair_of(n)
                    pe.wait_ge(chunk_out, g * (2 * CH) + (n - 1))
                    for k in range(UPC):
                        if first and c == 0:
                            pe.wait_ge(turn_lo, 2 * splits_before(T_X2) + k + 1)
                        if c == CH:
                            pe.wait_ge(turn_lo, g * (2 * CH) + (2 * splits_before(T_FF) + k + 1))
                        x_hi, x_lo = (a_hi, a_lo) if c < CH else (c_hi, c_lo)
                        unit(U_FF + UPC * c + k, r, x_hi, x_lo, 2 * k, 2 * p, k == 0, k == UPC - 1)
                        if first and c == 0 and k == 1:
                            pe.wait_ge(chunk_out, N_XO + CH)
                            turn(T_X2 + CH - 1, xres, NC * (CH - 1), split_out(T_X2 + CH - 2))
                        if k == 3 and 1 <= c <= CH:
                            pe.wait_ge(chunk_out, g * (2 * CH) + n)
                            turn(None, rows[:, pair_of(n - 1), :, :], 0,
                                 (turn_lo, g * (2 * CH) + (2 * splits_before(T_FF + c - 2) + 1)))

            ff_group(0, 0, True)
            with pe.Fori(1, GROUPS) as g:
                ff_group(g, g * FF_UNITS)


_INS = ['x', 'mem', 'positions', 'norm_mix_g', 'w_in', 'b_gate', 'conv_w', 'conv_b', 'conv_ln_g', 'conv_ln_b',
        'w_conv_out', 'q_norm_g', 'w_uq', 'kv_norm_g', 'w_ukv', 'w_mla_out', 'w_out', 'norm_mem_g', 'mem_norm_g',
        'w_xq', 'w_xkv', 'w_xo', 'norm_ffn_g', 'w_ff1', 'w_ff2', 'final_norm_g']
_OUTS = [((1, SEQ, D), 'float32')]


def kernel(**inputs):
    import numpy as _np
    import concourse.bacc as _bacc
    from concourse import mybir as _mybir
    from concourse.bass_utils import run_bass_kernel_spmd as _run

    nc = _bacc.Bacc("TRN2", target_bir_lowering=False, num_devices=1)
    arrays, args = {}, []
    for name in _INS:
        a = _np.ascontiguousarray(inputs[name])
        arrays[f"in_{name}_dram"] = a
        args.append(nc.dram_tensor(f"in_{name}_dram", a.shape, _mybir.dt.from_np(a.dtype), kind="ExternalInput").ap())
    for i, (shape, dtype) in enumerate(_OUTS):
        dt = _mybir.dt.from_np(_np.dtype(dtype))
        args.append(nc.dram_tensor(f"out_{i}_dram", shape, dt, kind="ExternalOutput").ap())
    build(nc, *args)
    r = _run(nc, [arrays], core_ids=[0])
    got = tuple(r.results[0][f"out_{i}_dram"] for i in range(len(_OUTS)))
    return got[0]
```
